# Optimizing a Trainium2 kernel written in Bass

```python
import math
import jax
import jax.numpy as jnp
from jax import lax
import numpy as np

D_MODEL = 1024
BATCH = 1
SEQ = 512
DEPTH = 2

CHUNK = 64
Q_BLOCK = 128
NORM_EPS = 1e-6
ROPE_THETA = 10000.0

DIFF_HEADS = 4
DIFF_QK_DIM = 64
DIFF_V_DIM = 128
MLA_HEADS = 4
MLA_Q_LORA = 384
MLA_KV_LORA = 256
MLA_NOPE = 64
MLA_ROPE = 32
MLA_V_DIM = 128
GDN_HEADS = 4
GDN_K_DIM = 128
GDN_V_DIM = 128
GDN_CONV = 4
FFN_HIDDEN = ((8 * D_MODEL // 3 + 255) // 256) * 256

N_BRANCHES = 3
IN_WIDTHS = (
    DIFF_HEADS * 2 * DIFF_QK_DIM,
    DIFF_HEADS * 2 * DIFF_QK_DIM,
    DIFF_HEADS * DIFF_V_DIM,
    MLA_Q_LORA,
    MLA_KV_LORA + MLA_ROPE,
    GDN_HEADS * GDN_K_DIM,
    GDN_HEADS * GDN_K_DIM,
    GDN_HEADS * GDN_V_DIM,
    GDN_HEADS * GDN_V_DIM,
    GDN_HEADS,
    GDN_HEADS,
    N_BRANCHES * D_MODEL,
)
IN_COLS = sum(IN_WIDTHS)
IN_OFFSETS = tuple(int(o) for o in np.cumsum(IN_WIDTHS)[:-1])

kernel_name = 'hybrid_diff_mla_gdn_streaming_block'

def _rms_norm(x, w):
    xf = x.astype(jnp.float32)
    y = xf * lax.rsqrt(jnp.mean(xf * xf, axis=-1, keepdims=True) + NORM_EPS)
    return (y * w.astype(jnp.float32)).astype(x.dtype)

def _l2_norm(x):
    xf = x.astype(jnp.float32)
    return xf * lax.rsqrt(jnp.sum(xf * xf, axis=-1, keepdims=True) + NORM_EPS)

def _rope(t, pos):
    half = t.shape[-1] // 2
    inv_freq = ROPE_THETA ** (-jnp.arange(half, dtype=jnp.float32) / half)
    ang = pos.astype(jnp.float32)[:, :, None, None] * inv_freq
    cos, sin = jnp.cos(ang), jnp.sin(ang)
    tf = t.astype(jnp.float32)
    t1, t2 = tf[..., :half], tf[..., half:]
    return jnp.concatenate([t1 * cos - t2 * sin, t2 * cos + t1 * sin], axis=-1).astype(t.dtype)

def _causal_dwconv(x, w):
    k_size, seq = w.shape[0], x.shape[1]
    xp = jnp.pad(x, ((0, 0), (k_size - 1, 0), (0, 0)))
    y = xp[:, 0:seq] * w[0]
    for i in range(1, k_size):
        y = y + xp[:, i:i + seq] * w[i]
    return y

def _chunk_causal_softmax(scores, q_start):
    n_keys = scores.shape[-1]
    q_chunk = (q_start + jnp.arange(Q_BLOCK)) // CHUNK
    k_chunk = jnp.arange(n_keys) // CHUNK
    allowed = k_chunk[None, :] <= q_chunk[:, None]
    return jax.nn.softmax(jnp.where(allowed, scores.astype(jnp.float32), -jnp.inf), axis=-1)

def _sweep_query_blocks(body, *qs):
    b, h, s = qs[0].shape[:3]
    nb = s // Q_BLOCK
    blocks = tuple(jnp.moveaxis(q.reshape(b, h, nb, Q_BLOCK, q.shape[-1]), 2, 0) for q in qs)
    out = lax.map(lambda a: body(a[0] * Q_BLOCK, *a[1]), (jnp.arange(nb), blocks))
    return jnp.moveaxis(out, 0, 2).reshape(b, h, s, out.shape[-1])

def _diff_attention(q, k, v, qn_w, kn_w, lam_p, subln_w, lambda_init):
    b, s = v.shape[:2]
    q = _rms_norm(q.reshape(b, s, DIFF_HEADS, 2, DIFF_QK_DIM), qn_w).transpose(0, 2, 3, 1, 4)
    k = _rms_norm(k.reshape(b, s, DIFF_HEADS, 2, DIFF_QK_DIM), kn_w).transpose(0, 2, 3, 1, 4)
    v = v.reshape(b, s, DIFF_HEADS, DIFF_V_DIM).transpose(0, 2, 1, 3)
    lp = lam_p.astype(jnp.float32)
    lam = jnp.exp(jnp.sum(lp[0] * lp[1])) - jnp.exp(jnp.sum(lp[2] * lp[3])) + lambda_init
    k1, k2 = k[:, :, 0], k[:, :, 1]
    scale = DIFF_QK_DIM ** -0.5

    def body(q_start, q1, q2):
        s1 = jnp.einsum('bhqd,bhkd->bhqk', q1, k1, preferred_element_type=jnp.float32) * scale
        s2 = jnp.einsum('bhqd,bhkd->bhqk', q2, k2, preferred_element_type=jnp.float32) * scale
        p = _chunk_causal_softmax(s1, q_start) - lam * _chunk_causal_softmax(s2, q_start)
        return jnp.einsum('bhqk,bhkd->bhqd', p.astype(v.dtype), v)

    o = _sweep_query_blocks(body, q[:, :, 0], q[:, :, 1])
    o = _rms_norm(o, subln_w) * (1.0 - lambda_init)
    return o.transpose(0, 2, 1, 3).reshape(b, s, DIFF_HEADS * DIFF_V_DIM)

def _mla(q_lat, kv_lat, pos, qa_w, q_up, kva_w, kv_up, qn_w, kn_w):
    b, s = q_lat.shape[:2]
    qk_dim = MLA_NOPE + MLA_ROPE
    q = (_rms_norm(q_lat, qa_w) @ q_up).reshape(b, s, MLA_HEADS, qk_dim)
    c_kv, k_rope = kv_lat[..., :MLA_KV_LORA], kv_lat[..., MLA_KV_LORA:]
    kv = (_rms_norm(c_kv, kva_w) @ kv_up).reshape(b, s, MLA_HEADS, MLA_NOPE + MLA_V_DIM)
    k_nope, v = kv[..., :MLA_NOPE], kv[..., MLA_NOPE:]
    k = jnp.concatenate(
        [k_nope, jnp.broadcast_to(k_rope[:, :, None, :], (b, s, MLA_HEADS, MLA_ROPE))], axis=-1)
    q = _rms_norm(q, qn_w)
    k = _rms_norm(k, kn_w)
    q = jnp.concatenate([q[..., :MLA_NOPE], _rope(q[..., MLA_NOPE:], pos)], axis=-1).transpose(0, 2, 1, 3)
    k = jnp.concatenate([k[..., :MLA_NOPE], _rope(k[..., MLA_NOPE:], pos)], axis=-1).transpose(0, 2, 1, 3)
    v = v.transpose(0, 2, 1, 3)
    scale = qk_dim ** -0.5

    def body(q_start, qb):
        sc = jnp.einsum('bhqd,bhkd->bhqk', qb, k, preferred_element_type=jnp.float32) * scale
        p = _chunk_causal_softmax(sc, q_start)
        return jnp.einsum('bhqk,bhkd->bhqd', p.astype(v.dtype), v)

    o = _sweep_query_blocks(body, q)
    return o.transpose(0, 2, 1, 3).reshape(b, s, MLA_HEADS * MLA_V_DIM)

def _chunk_gated_delta_rule(q, k, v, g, beta):
    b, s, h, dk = q.shape
    dv = v.shape[-1]
    n = s // CHUNK

    def chunks(t):
        t = t.reshape(b, n, CHUNK, h, *t.shape[3:])
        return jnp.moveaxis(jnp.swapaxes(t, 2, 3), 1, 0)

    q, k, v, g, beta = (chunks(t) for t in (q, k, v, g, beta))
    g = jnp.cumsum(g, axis=-1)
    idx = jnp.arange(CHUNK)
    incl = idx[:, None] >= idx[None, :]
    strict = idx[:, None] > idx[None, :]
    decay = jnp.exp(jnp.where(incl, g[..., :, None] - g[..., None, :], -jnp.inf))
    k_beta = k * beta[..., None]
    lower = jnp.where(strict, jnp.einsum('nbhid,nbhjd->nbhij', k_beta, k) * decay, 0.0)
    eye = jnp.eye(CHUNK, dtype=jnp.float32)
    t_mat = lax.linalg.triangular_solve(lower + eye, jnp.broadcast_to(eye, lower.shape),
                                        left_side=True, lower=True, unit_diagonal=True)
    u = t_mat @ (v * beta[..., None])
    w = t_mat @ (k_beta * jnp.exp(g)[..., None])
    attn = jnp.where(incl, jnp.einsum('nbhid,nbhjd->nbhij', q, k) * decay, 0.0)

    def step(state, inp):
        q_n, k_n, u_n, w_n, g_n, a_n = inp
        v_new = u_n - jnp.einsum('bhcd,bhde->bhce', w_n, state)
        o = (jnp.einsum('bhcd,bhde->bhce', q_n * jnp.exp(g_n)[..., None], state)
             + jnp.einsum('bhij,bhje->bhie', a_n, v_new))
        g_last = g_n[..., -1]
        state = (state * jnp.exp(g_last)[..., None, None]
                 + jnp.einsum('bhcd,bhce->bhde', k_n * jnp.exp(g_last[..., None] - g_n)[..., None], v_new))
        return state, o

    state0 = jnp.zeros((b, h, dk, dv), jnp.float32)
    _, o = lax.scan(step, state0, (q, k, u, w, g, attn))
    return jnp.swapaxes(jnp.moveaxis(o, 0, 1), 2, 3).reshape(b, s, h, dv)

def _gated_deltanet(q, k, v, z, beta_logit, a, conv_w, a_log, dt_bias, onorm_w):
    b, s = q.shape[:2]
    qk_w = GDN_HEADS * GDN_K_DIM
    qkv = jax.nn.silu(_causal_dwconv(jnp.concatenate([q, k, v], axis=-1), conv_w))
    q, k, v = jnp.split(qkv, [qk_w, 2 * qk_w], axis=-1)
    q = _l2_norm(q.reshape(b, s, GDN_HEADS, GDN_K_DIM)) * GDN_K_DIM ** -0.5
    k = _l2_norm(k.reshape(b, s, GDN_HEADS, GDN_K_DIM))
    v = v.reshape(b, s, GDN_HEADS, GDN_V_DIM).astype(jnp.float32)
    beta = jax.nn.sigmoid(beta_logit.astype(jnp.float32))
    g = -jnp.exp(a_log.astype(jnp.float32)) * jax.nn.softplus(a.astype(jnp.float32) + dt_bias.astype(jnp.float32))
    o = _chunk_gated_delta_rule(q, k, v, g, beta)
    o = _rms_norm(o, onorm_w) * jax.nn.silu(z.reshape(b, s, GDN_HEADS, GDN_V_DIM).astype(jnp.float32))
    return o.reshape(b, s, GDN_HEADS * GDN_V_DIM).astype(z.dtype)

def _swiglu(h, w_gu, w_down):
    gate, up = jnp.split(h @ w_gu, 2, axis=-1)
    return (jax.nn.silu(gate) * up) @ w_down

def setup_inputs(seed: int = 0) -> dict:
    key = jax.random.key(seed)
    keys = list(jax.random.split(key, 40))
    f32 = jnp.float32

    def normal(shape, fan_in, gain=1.0):
        return jax.random.normal(keys.pop(), shape, f32) * (gain * fan_in ** -0.5)

    def gain(d):
        return 1.0 + 0.1 * jax.random.normal(keys.pop(), (DEPTH, d), f32)

    offsets = jax.random.randint(keys.pop(), (BATCH, 1), 0, 64) * CHUNK
    positions = (offsets + jnp.arange(SEQ)[None, :]).astype(jnp.int32)
    dt = jnp.exp(jax.random.uniform(keys.pop(), (DEPTH, GDN_HEADS), f32,
                                    minval=math.log(1e-3), maxval=math.log(1e-1)))
    return {
        'x': jax.random.normal(keys.pop(), (BATCH, SEQ, D_MODEL), f32),
        'c': jax.random.normal(keys.pop(), (BATCH, D_MODEL), f32),
        'positions': positions,
        'ada_w': normal((DEPTH, D_MODEL, 6 * D_MODEL), D_MODEL, 0.5),
        'ada_b': 0.02 * jax.random.normal(keys.pop(), (DEPTH, 6 * D_MODEL), f32),
        'norm1_w': gain(D_MODEL),
        'w_in': normal((DEPTH, D_MODEL, IN_COLS), D_MODEL),
        'diff_qnorm_w': gain(DIFF_QK_DIM),
        'diff_knorm_w': gain(DIFF_QK_DIM),
        'diff_lambda': 0.1 * jax.random.normal(keys.pop(), (DEPTH, 4, DIFF_QK_DIM), f32),
        'diff_subln_w': gain(DIFF_V_DIM),
        'w_o_diff': normal((DEPTH, DIFF_HEADS * DIFF_V_DIM, D_MODEL), DIFF_HEADS * DIFF_V_DIM),
        'mla_qa_norm_w': gain(MLA_Q_LORA),
        'mla_q_up': normal((DEPTH, MLA_Q_LORA, MLA_HEADS * (MLA_NOPE + MLA_ROPE)), MLA_Q_LORA),
        'mla_kva_norm_w': gain(MLA_KV_LORA),
        'mla_kv_up': normal((DEPTH, MLA_KV_LORA, MLA_HEADS * (MLA_NOPE + MLA_V_DIM)), MLA_KV_LORA),
        'mla_qnorm_w': gain(MLA_NOPE + MLA_ROPE),
        'mla_knorm_w': gain(MLA_NOPE + MLA_ROPE),
        'w_o_mla': normal((DEPTH, MLA_HEADS * MLA_V_DIM, D_MODEL), MLA_HEADS * MLA_V_DIM),
        'gdn_conv_w': normal((DEPTH, GDN_CONV, GDN_HEADS * (2 * GDN_K_DIM + GDN_V_DIM)), GDN_CONV),
        'gdn_a_log': jnp.log(jax.random.uniform(keys.pop(), (DEPTH, GDN_HEADS), f32, minval=1.0, maxval=16.0)),
        'gdn_dt_bias': dt + jnp.log(-jnp.expm1(-dt)),
        'gdn_onorm_w': gain(GDN_V_DIM),
        'w_o_gdn': normal((DEPTH, GDN_HEADS * GDN_V_DIM, D_MODEL), GDN_HEADS * GDN_V_DIM),
        'w_out': normal((DEPTH, D_MODEL, D_MODEL), D_MODEL),
        'norm2_w': gain(D_MODEL),
        'ffn_w_gu': normal((DEPTH, D_MODEL, 2 * FFN_HIDDEN), D_MODEL),
        'ffn_w_down': normal((DEPTH, FFN_HIDDEN, D_MODEL), FFN_HIDDEN),
    }

def reference(x, c, positions, ada_w, ada_b, norm1_w, w_in, diff_qnorm_w, diff_knorm_w,
              diff_lambda, diff_subln_w, w_o_diff, mla_qa_norm_w, mla_q_up, mla_kva_norm_w,
              mla_kv_up, mla_qnorm_w, mla_knorm_w, w_o_mla, gdn_conv_w, gdn_a_log, gdn_dt_bias,
              gdn_onorm_w, w_o_gdn, w_out, norm2_w, ffn_w_gu, ffn_w_down):
    for l in range(DEPTH):
        lambda_init = 0.8 - 0.6 * math.exp(-0.3 * l)
        mod = (c @ ada_w[l] + ada_b[l])[:, None, :]
        sh1, sc1, g1, sh2, sc2, g2 = jnp.split(mod, 6, axis=-1)

        h = _rms_norm(x, norm1_w[l]) * (1.0 + sc1) + sh1
        (a_q, a_k, a_v, b_q, b_kv, c_q, c_k, c_v, c_z, c_b, c_a,
         gate_logits) = jnp.split(h @ w_in[l], IN_OFFSETS, axis=-1)
        y_a = _diff_attention(a_q, a_k, a_v, diff_qnorm_w[l], diff_knorm_w[l], diff_lambda[l],
                              diff_subln_w[l], lambda_init) @ w_o_diff[l]
        y_b = _mla(b_q, b_kv, positions, mla_qa_norm_w[l], mla_q_up[l], mla_kva_norm_w[l],
                   mla_kv_up[l], mla_qnorm_w[l], mla_knorm_w[l]) @ w_o_mla[l]
        y_c = _gated_deltanet(c_q, c_k, c_v, c_z, c_b, c_a, gdn_conv_w[l], gdn_a_log[l],
                              gdn_dt_bias[l], gdn_onorm_w[l]) @ w_o_gdn[l]
        gate_a, gate_b, gate_c = jnp.split(jax.nn.sigmoid(gate_logits), N_BRANCHES, axis=-1)
        merged = gate_a * y_a + gate_b * y_b + gate_c * y_c
        x = x + g1 * (merged @ w_out[l])

        h = _rms_norm(x, norm2_w[l]) * (1.0 + sc2) + sh2
        x = x + g2 * _swiglu(h, ffn_w_gu[l], ffn_w_down[l])
    return x


_drawn_inputs = setup_inputs


def setup_inputs(seed=0):
    import zlib

    import numpy as np

    out = dict(_drawn_inputs(seed))
    spreads = {}
    factors = {'diff_qnorm_w': 6.983,
     'diff_knorm_w': 6.704,
     'diff_lambda': 6.506,
     'mla_qa_norm_w': 8.0,
     'mla_kva_norm_w': 3.145,
     'mla_qnorm_w': 8.0,
     'mla_knorm_w': 8.0}
    for name, (base, spread) in spreads.items():
        noise = np.random.default_rng([zlib.crc32(name.encode()), seed]).standard_normal(out[name].shape)
        drawn = base * np.exp(spread * noise) if base else spread * noise
        out[name] = jnp.asarray(drawn.astype(out[name].dtype))
    for name, factor in factors.items():
        out[name] = (out[name] * factor).astype(out[name].dtype)
    return out
```

```python
from contextlib import ExitStack

import numpy as np
import concourse.bass as bass
from concourse import mybir

F32 = mybir.dt.float32
F32R = mybir.dt.float32r
I32 = mybir.dt.int32
ALU = mybir.AluOpType
ACT = mybir.ActivationFunctionType
AX = mybir.AxisListType

P = 128
D = 1024
T = 512
KD = D // P
NT = T // P
DEPTH = 2
CHUNK = 64
REGION = 128
EPS = 1e-6
QK = 64
MQK = 96
F = 2816
KF = F // P
RAW_SLOTS = 4
SPLIT_SLOTS = 2
ADA_COLS = 6 * KD
ADA_GROUPS = 6 * D // T
ADA_FIRST = 2 * D // T
ADA_REST = ADA_GROUPS - ADA_FIRST
ADA_SLOTS = 4
ADA1_SLOTS = 5

U_CONV = 0
U_Z = U_CONV + 12
U_DV = U_Z + 4
U_BA = U_DV + 4
U_DIFF = U_BA + 1
U_GATE_C = U_DIFF + 8
U_PROJ_C = U_GATE_C + KD
U_LAT = U_PROJ_C + KD // 2
U_QUP = U_LAT + 6
U_KUP = U_QUP + 2
U_VUP = U_KUP + 1
U_GATE_A = U_VUP + 1
U_PROJ_A = U_GATE_A + KD
U_GATE_B = U_PROJ_A + KD // 2
U_PROJ_B = U_GATE_B + KD
U_OUT = U_PROJ_B + KD // 2
U_GU = U_OUT + 8
U_DOWN = U_GU + 2 * KF
UNITS = U_DOWN + 3 * KD
UNITS_PAD = -(-UNITS // RAW_SLOTS) * RAW_SLOTS

MQK_LAST = (1, 3, 7)
SUB_FILL = (4, 4, 3, 2)
ADA_SUM_AFTER = (5, 7, 10, 13, 14, 15)
PARAMS = {}
_at = 0
for _name, _n in (("norm1", 8), ("norm2", 8), ("ada_b", 48), ("diff_q", 1), ("diff_k", 1), ("subln", 1),
                  ("qa", 3), ("kva", 2), ("mla_q", 1), ("mla_k", 1), ("conv", 48), ("onorm", 1),
                  ("lambda", 4), ("lambda_init", 1), ("one_minus_init", 1), ("a_log", 16), ("dt_bias", 16)):
    PARAMS[_name] = (_at, _at + _n)
    _at += _n
NPARAM = _at

CONSTS = ["ident", "ones", "blockones", "rot", "tri", "suffix", "first", "second", "negmask", "negmask2",
          "lvl1", "lvl2", "lvl4", "lvl8", "lvl16", "lvl32"]
LEVELS = (2, 4, 8, 16, 32)


class Background:

    def __init__(self):
        self.pieces = 0
        self.made = {}
        self.at = {}

    def fill(self, work, place, n):
        for _ in range(n):
            if next(work, "end") == "end":
                break
            self.pieces += 1
        self.at[place] = self.pieces

    def mark(self, what):
        self.made[what] = self.pieces + 1


class Follower:
    def __init__(self, bg, work):
        self.bg, self.work = bg, work
        self.need = next(work, None)

    def upto(self, place):
        while self.need is not None and self.need <= self.bg.at[place]:
            self.need = next(self.work, None)

    def finish(self):
        while self.need is not None:
            self.need = next(self.work, None)


def build(nc, x_in, wpack, apack, c_in, params_in, consts_in, freq_in, pos_in, x_spill, out):
    with ExitStack() as ctx:
        K = 1024
        base = [18560]

        def fixed(name, shape, dt=F32):
            n = int(np.prod(shape[1:])) * 4
            t = nc.alloc_sbuf_tensor_at(name, list(shape), dt, offset=base[0])
            base[0] += -(-n // 32) * 32
            return t

        h_hi = fixed("h_hi", [P, KD, T], F32R)
        h_lo = fixed("h_lo", [P, KD, T], F32R)
        raw = [fixed(f"raw{i}", [P, 8, P]) for i in range(RAW_SLOTS)]
        w_hi = [fixed(f"w_hi{i}", [P, 8, P], F32R) for i in range(SPLIT_SLOTS)]
        w_lo = [fixed(f"w_lo{i}", [P, 8, P], F32R) for i in range(SPLIT_SLOTS)]
        consts = fixed("consts", [P, len(CONSTS), P])
        par = fixed("par", [P, NPARAM])
        c_col = fixed("c_col", [P, KD])
        freq = fixed("freq", [P, 1])
        cos = fixed("cos", [P, T])
        sin = fixed("sin", [P, T])
        mod = fixed("mod", [P, ADA_COLS])
        mod_raw = fixed("mod_raw", [P, 4 * ADA_FIRST])
        normA = fixed("normA", [P, 2, KD])
        half_g = fixed("half_g", [P, 2, KD])
        small = fixed("small", [P, 144])
        biases = fixed("biases", [P, 4])
        gate_op = fixed("gate_op", [P, 1])
        R0 = base[0]
        assert R0 + REGION * K <= 229344, R0 + REGION * K

        def region(name, kib, shape, dt=F32):
            assert kib * K + int(np.prod(shape[1:])) * 4 <= REGION * K, name
            return nc.alloc_sbuf_tensor_at(name, list(shape), dt, offset=R0 + int(kib * K))

        x = region("x", 112, [P, KD, T])
        sqx2 = region("sqx2", 16, [P, T])
        ssq2 = region("ssq2", 26, [P, T])
        tn = region("tn", 20, [P, 2, T])
        rn = region("rn", 24, [P, T])
        ssq = region("ssq", 88, [P, T])
        sqx = region("sqx", 90, [P, T])
        qkv = region("qkv", 0, [P, 12, T])
        z_t = region("z_t", 24, [P, 4, T])
        vb = region("vb", 32, [P, 4, P])
        kb = region("kb", 34, [P, 4, P])
        kd = region("kd", 36, [P, 4, P])
        at_ = region("at_", 38, [P, 4, P])
        wt = region("wt", 40, [P, 4, P])
        Y = region("Y", 42, [P, 4, P])
        qg = region("qg", 44, [P, 4, P])
        dt_ = region("dt_", 46, [P, 4, P])
        lt = region("lt", 48, [P, 4, P])
        X = region("X", 50, [P, 4, P])
        pm = region("pm", 52, [P, 4, P])
        bt = region("bt", 54, [P, 4, P])
        S = region("S", 56, [P, 2, 4, P])
        vn = region("vn", 60, [P, 4, P])
        gb = region("gb", 62, [P, 4, P])
        eg = region("eg", 62, [P, 4, P])
        bb = region("bb", 64, [P, 4, P])
        gsmall = region("gsmall", 66, [P, 128])
        sqa = region("sqa", 67, [P, T])
        ra = region("ra", 69, [P, T])
        sqg = region("sqg", 46, [P, 2, T])
        rg = region("rg", 50, [P, 2, T])
        craw = region("craw", 71, [P, 2, T + 3])
        cy = region("cy", 76, [P, 2, T])
        ct = region("ct", 80, [P, 2, T])
        ada_acc = region("ada_acc", 60, [P, 2, T])
        ada1 = [region(f"ada1_{i}", 40 + 4 * i, [P, 2, T]) for i in range(ADA1_SLOTS)]
        ba_rows = region("ba_rows", 84, [P, T])
        gates = region("gates", 95, [P, KD, T])
        dqkv = region("dqkv", 71, [P, 12, T])
        merged = region("merged", 0, [P, KD, T])
        lat = region("lat", 16, [P, 6, T])
        mv = region("mv", 16, [P, 4, T])
        sqd = region("sqd", 38, [P, 2, T])
        rd = region("rd", 42, [P, 2, T])
        sqm = region("sqm", 28, [P, 2, T])
        rm = region("rm", 32, [P, 2, T])
        lat_lo = region("lat_lo", 38, [P, 5, T], F32R)
        lat_hi = region("lat_hi", 112, [P, 5, T], F32R)
        my = region("my", 122, [P, 2, T])
        probs = region("probs", 48, [P, 2, 2, T])
        pt = region("pt", 56, [P, 2, NT, P])
        oraw = region("oraw", 60, [P, 4, T])
        mask_row = region("mask_row", 36, [P, P + CHUNK], F32R)
        sqo = region("sqo", 28, [P, 2, T])
        ro = region("ro", 32, [P, 2, T])
        oy = region("oy", 38, [P, 2, T])
        mq = region("mq", 95, [P, 8, T])
        o_hi = region("o_hi", 112, [P, 4, T], F32R)
        o_lo = region("o_lo", 120, [P, 4, T], F32R)
        mprobs = region("mprobs", 24, [P, 2, T])
        mpt = region("mpt", 28, [P, 2, NT, P])
        gyb = region("gyb", 32, [P, 2, T])
        ob_hi = region("ob_hi", 44, [P, 4, T], F32R)
        ob_lo = region("ob_lo", 52, [P, 4, T], F32R)
        gates2 = region("gates2", 76, [P, KD, T])
        m_hi = region("m_hi", 60, [P, KD, T], F32R)
        m_lo = region("m_lo", 92, [P, KD, T], F32R)
        hid_hi = region("hid_hi", 0, [P, KF, T], F32R)
        hid_lo = region("hid_lo", 44, [P, KF, T], F32R)
        ft = region("ft", 88, [P, 2, T])
        fy = region("fy", 92, [P, 2, T])
        ada_acc2 = region("ada_acc2", 92, [P, T])
        ada2 = [region(f"ada2_{i}", 96 + 4 * i, [P, 2, T]) for i in range(4)]
        pos_i = region("pos_i", 80, [P, T], I32)
        ang = region("ang", 82, [P, T])
        turns = region("turns", 84, [P, T])
        red = region("red", 86, [P, T])
        ada0 = region("ada0", 0, [P, 4 * ADA_FIRST, 2, T])
        ada_acc0 = region("ada_acc0", 64, [P, 2, T])

        G = [nc.alloc_psum_tensor(f"bank{i}", [P, T], F32) for i in range(8)]

        sems = {}

        def sem(name):
            if name not in sems:
                sems[name] = ctx.enter_context(nc.semaphore(name))
            return sems[name]


        def C(name):
            return consts[:, CONSTS.index(name), :]

        def PAR(name, i=0, n=1):
            a = PARAMS[name][0] + i
            return par[:, a:a + n]

        eps = biases[:, 0:1]
        ln_half = biases[:, 1:2]
        ln_half_q = biases[:, 2:3]

        sm = {}
        at = [0]

        def cols(name, n):
            sm[name] = small[:, at[0]:at[0] + n]
            at[0] += n
            assert at[0] <= small.shape[1]
            return sm[name]

        gat = [0]

        def gcols(name, n):
            gat[0] += n
            assert gat[0] <= gsmall.shape[1]
            return gsmall[:, gat[0] - n:gat[0]]

        lam_p = cols("lam_p", 2)
        lam_e = cols("lam_e", 2)
        neg_lam = cols("neg_lam", 1)
        subw = cols("subw", 1)
        ba = gcols("ba", 32)
        beta = cols("beta", 16)
        beta_half = gcols("beta_half", 16)
        sp_abs = gcols("sp_abs", 16)
        sp_relu = gcols("sp_relu", 16)
        gdec = cols("gdec", 16)
        ealog = gcols("ealog", 16)
        gcol = gcols("gcol", 16)
        dec = cols("dec", 64)
        e_g = dec[:, 0:16]
        e_suf = dec[:, 16:32]
        e_tot = [dec[:, 32:48], dec[:, 48:64]]
        beta_eg = cols("beta_eg", 16)
        mx = cols("mx", 4)
        nm = cols("nm", 4)
        rs = cols("rs", 4)
        rr = cols("rr", 4)

        def group(ap, width):
            n = ap.shape[1]
            return ap.unsqueeze(2).broadcast_to([P, n, width])

        def heads(ap):
            return ap.unsqueeze(1).broadcast_to([P, 4, P])

        first = ExitStack()
        once_sem = lambda name: first.enter_context(nc.semaphore(name))
        s_first_loads = once_sem("positions_frequencies_c_loaded")
        s_x_in = once_sem("x_in_loaded")
        s_consts_in = once_sem("consts_loaded")
        s_ada0_in = [once_sem(f"ada0_loaded{g}") for g in range(ADA_FIRST)]
        s_ones = once_sem("ones_column")
        s_angle_step = once_sem("angle_step")
        s_ada0 = once_sem("ada0_step")
        s_ada0_mm = once_sem("ada0_mm")
        s_pool_once = once_sem("pool_step")
        s_angles = once_sem("angles_reduced")
        s_tables = once_sem("tables_made")
        with nc.Block() as once:
            @once.sync
            def _(sp):
                sp.dma_start(pos_i[:], pos_in.broadcast_to([P, T])).then_inc(s_first_loads, 16)
                sp.dma_start(freq[:], freq_in).then_inc(s_first_loads, 16)
                sp.dma_start(c_col[:], c_in).then_inc(s_first_loads, 16)
                for g in range(ADA_FIRST):
                    first_part = 4 * (ADA_REST + g)
                    sp.dma_start(ada0[:, 4 * g:4 * g + 4], apack[DEPTH - 1, first_part:first_part + 4].rearrange(
                        "n p b t -> p n b t")).then_inc(s_ada0_in[g], 16)
                    if g == 0:
                        sp.dma_start(x[:], x_in).then_inc(s_x_in, 16)
                sp.dma_start(consts[:], consts_in).then_inc(s_consts_in, 16)

            @once.tensor
            def _(pe):
                pe.wait_ge(s_ones, 1)
                for g in range(ADA_FIRST):
                    pe.wait_ge(s_ada0, 8 * g + 8)
                    for b in range(4):
                        ins = nc.tensor.matmul(G[7][:, 4 * g + b:4 * g + b + 1], ada_acc0[:, g % 2, b * P:b * P + P],
                                               biases[:, 3:4], start=True, stop=True)
                    ins.then_inc(s_ada0_mm, 1)
                pe.wait_ge(s_consts_in, 16)

            @once.vector
            def _(dve):
                dve.wait_ge(s_first_loads, 48)
                dve.memset(biases[:, 3:4], 1.0).then_inc(s_ones, 1)
                dve.memset(biases[:, 0:1], EPS)
                dve.memset(biases[:, 1:2], float(np.log(0.5)))
                dve.memset(biases[:, 2:3], float(np.log(0.5) - 0.5 * np.log(128.0)))
                n = [0]

                def link(ins):
                    n[0] += 1
                    ins.then_inc(s_angle_step, 1)
                    dve.wait_ge(s_angle_step, n[0])

                link(dve.tensor_copy(ang[:], pos_i[:]))
                link(dve.tensor_scalar(ang[:], ang[:], freq[:, 0:1], None, ALU.mult))
                big = 1.5 * 2.0 ** 23
                link(dve.tensor_scalar(turns[:], ang[:], float(1 / (2 * np.pi)), big, ALU.mult, ALU.add))
                link(dve.tensor_scalar(turns[:], turns[:], big, None, ALU.subtract))
                c1 = 6.28125
                c2 = float(np.float32(np.round((2 * np.pi - c1) * 2 ** 20) / 2 ** 20))
                c3 = float(2 * np.pi - c1 - c2)
                for c in (c1, c2, c3):
                    link(dve.scalar_tensor_tensor(out=ang[:], in0=turns[:], scalar=-c, in1=ang[:],
                                                  op0=ALU.mult, op1=ALU.add))
                link(dve.tensor_scalar(ang[:], ang[:], float(np.float32(3.1415925)), float(np.float32(-3.1415925)),
                                       ALU.min, ALU.max))
                link(dve.tensor_scalar(red[:], ang[:], -1.0, None, ALU.mult))
                link(dve.tensor_tensor(red[:], red[:], ang[:], ALU.max))
                dve.tensor_scalar(red[:], red[:], -1.0, float(np.pi / 2), ALU.mult, ALU.add).then_inc(s_angles, 1)
                for g in range(ADA_FIRST):
                    acc = ada_acc0[:, g % 2, :]
                    dve.wait_ge(s_ada0_in[g], 16)
                    if g >= 2:
                        dve.wait_ge(s_ada0_mm, g - 1)
                    for k in range(KD):
                        part = ada0[:, 4 * g + k // 2, k % 2, :]
                        if k == 0:
                            dve.tensor_scalar(acc, part, c_col[:, 0:1], None, ALU.mult).then_inc(s_ada0, 1)
                        else:
                            dve.scalar_tensor_tensor(out=acc, in0=part, scalar=c_col[:, k:k + 1], in1=acc,
                                                     op0=ALU.mult, op1=ALU.add).then_inc(s_ada0, 1)
                        dve.wait_ge(s_ada0, 8 * g + k + 1)
                dve.wait_ge(s_ada0_mm, ADA_FIRST)
                dve.tensor_copy(mod_raw[:, 0:4 * ADA_FIRST], G[7][:, 0:4 * ADA_FIRST])

            @once.gpsimd
            def _(pool):
                n = [0]

                def link(ins):
                    n[0] += 1
                    ins.then_inc(s_pool_once, 1)
                    pool.wait_ge(s_pool_once, n[0])

                pool.wait_ge(s_x_in, 16)
                for k in range(KD):
                    link(pool.tensor_tensor(sqx[:] if k else ssq[:], x[:, k, :], x[:, k, :], ALU.mult))
                    if k:
                        link(pool.tensor_tensor(ssq[:], ssq[:], sqx[:], ALU.add))

            @once.scalar
            def _(act):
                act.wait_ge(s_angles, 1)
                nc.scalar.activation(sin[:], ang[:], ACT.Sin).then_inc(s_tables, 1)
                nc.scalar.activation(cos[:], red[:], ACT.Sin).then_inc(s_tables, 1)
                act.wait_ge(s_tables, 2)
                act.preload_act_table_set("natural_log_exp_and_others")

        nc.sync.sem_clear(range(s_first_loads.num, s_tables.num + 1))
        nc.all_engine_barrier()
        first.close()

        s_ada2_mm = sem("ada2_mm")
        s_ada2_step = sem("ada2_step")
        s_ada_mm = sem("ada_mm")
        s_ada_used = sem("ada_used")
        s_alog_exp = sem("alog_exp")
        s_at_made = sem("at_made")
        s_ba_raw = sem("ba_raw")
        s_ba_rows = sem("ba_rows")
        s_ba_tr = sem("ba_tr")
        s_beta_tanh = sem("beta_tanh")
        s_branch_o = sem("branch_o")
        s_bt_made = sem("bt_made")
        s_bx_mm = sem("bx_mm")
        s_bx_out = sem("bx_out")
        s_conv_out = sem("conv_out")
        s_conv_raw = sem("conv_raw")
        s_conv_tanh = sem("conv_tanh")
        s_conv_y = sem("conv_y")
        s_conv_y0 = sem("conv_y0")
        s_craw_zero = sem("craw_zero")
        s_d_made = sem("d_made")
        s_da_o = sem("da_o")
        s_da_pv = sem("da_pv")
        s_dec_cols = sem("dec_cols")
        s_dqk_mm = sem("dqk_mm")
        s_dqk_out = sem("dqk_out")
        s_dqk_r = sem("dqk_r")
        s_dqk_sq = sem("dqk_sq")
        s_dt_exp = sem("dt_exp")
        s_dv_out = sem("dv_out")
        s_eg_made = sem("eg_made")
        s_ffn_hi = sem("ffn_hi")
        s_ffn_lo = sem("ffn_lo")
        s_ffn_tanh = sem("ffn_tanh")
        s_ffn_y = sem("ffn_y")
        s_ffn_y2 = sem("ffn_y2")
        s_g_ready = sem("g_ready")
        s_gate2_tanh = sem("gate2_tanh")
        s_gate_merge = sem("gate_merge")
        s_gate_out = sem("gate_out")
        s_gate_raw = sem("gate_raw")
        s_gate_tanh = sem("gate_tanh")
        s_gcol = sem("gcol")
        s_gsum_mm = sem("gsum_mm")
        s_h_hi = sem("h_hi")
        s_h_lo = sem("h_lo")
        s_kb_made = sem("kb_made")
        s_kk_mm = sem("kk_mm")
        s_l2_done = sem("l2_done")
        s_l2_mm = sem("l2_mm")
        s_l2_r = sem("l2_r")
        s_l2_sq = sem("l2_sq")
        s_lam_exp = sem("lam_exp")
        s_lam_mm = sem("lam_mm")
        s_lam_prod = sem("lam_prod")
        s_lat_lo = sem("lat_lo")
        s_lat_mm = sem("lat_mm")
        s_lat_out = sem("lat_out")
        s_lat_r = sem("lat_r")
        s_lat_sq = sem("lat_sq")
        s_lt_made = sem("lt_made")
        s_m_lo = sem("m_lo")
        s_ma_exp = sem("ma_exp")
        s_ma_hi = sem("ma_hi")
        s_ma_o = sem("ma_o")
        s_ma_pv = sem("ma_pv")
        s_mask_made = sem("mask_made")
        s_mod_next = sem("mod_next")
        s_mod_ready = sem("mod_ready")
        s_mqk_cos = sem("mqk_cos")
        s_mqk_mm = sem("mqk_mm")
        s_mqk_r = sem("mqk_r")
        s_mqk_rope = sem("mqk_rope")
        s_mqk_rot = sem("mqk_rot")
        s_mqk_sq = sem("mqk_sq")
        s_mqk_ss = sem("mqk_ss")
        s_mqk_y = sem("mqk_y")
        s_mv_mm = sem("mv_mm")
        s_mv_out = sem("mv_out")
        s_norm_mm = sem("norm_mm")
        s_norm_r = sem("norm_r")
        s_norm_t = sem("norm_t")
        s_o_mm = sem("o_mm")
        s_o_out = sem("o_out")
        s_on_mm = sem("on_mm")
        s_on_r = sem("on_r")
        s_on_sq = sem("on_sq")
        s_on_y = sem("on_y")
        s_params_loaded = sem("params_loaded")
        s_proj_even = sem("proj_even")
        s_pty_mm = sem("pty_mm")
        s_qg_made = sem("qg_made")
        s_row_mm = sem("row_mm")
        s_rows_bcast = sem("rows_bcast")
        s_scalar_step = sem("scalar_step")
        s_sp_abs = sem("sp_abs")
        s_sp_ln = sem("sp_ln")
        s_split_hi = sem("split_hi")
        s_split_lo = sem("split_lo")
        s_ssq = sem("ssq")
        s_state = sem("state")
        s_su_mm = sem("su_mm")
        s_sub_mm = sem("sub_mm")
        s_sub_r = sem("sub_r")
        s_sub_sq = sem("sub_sq")
        s_sub_y = sem("sub_y")
        s_unit_used = sem("unit_used")
        s_vb_made = sem("vb_made")
        s_vector_step = sem("vector_step")
        s_vk_tr = sem("vk_tr")
        s_vn_made = sem("vn_made")
        s_vn_mm = sem("vn_mm")
        s_w_mm = sem("w_mm")
        s_w_out = sem("w_out")
        s_x_back = sem("x_back")
        s_x_made = sem("x_made")
        s_x_mid = sem("x_mid")
        s_x_new = sem("x_new")
        s_x_spilled = sem("x_spilled")
        s_x_sq = sem("x_sq")
        s_x_ssq = sem("x_ssq")
        s_x_tr = sem("x_tr")
        s_y_made = sem("y_made")
        s_yp_mm = sem("yp_mm")
        s_z_gated = sem("z_gated")
        s_z_tanh = sem("z_tanh")
        s_ada1_loaded = [sem(f"ada1_loaded{i}") for i in range(ADA1_SLOTS)]
        s_ada2_loaded = [sem(f"ada2_loaded{i}") for i in range(ADA_SLOTS)]
        s_raw_loaded = [sem(f"raw_loaded{i}") for i in range(RAW_SLOTS)]
        f_da = {k: sem(f"da_{k}") for k in ('exp', 'nm', 'o', 'p', 'pt', 'pv', 'qk', 'tr')}
        f_ma = {k: sem(f"ma_{k}") for k in ('exp', 'nm', 'o', 'p', 'pt', 'pv', 'qk', 'tr')}

        with nc.Fori(0, DEPTH) as layer:
            with nc.Block() as block:
                mix = Background()
                diff = Background()
                mla = Background()

                @block.sync
                def _(sp):
                    sp.dma_start(par[:], params_in[layer]).then_inc(s_params_loaded, 16)
                    for s in range(RAW_SLOTS):
                        sp.dma_start(raw[s][:], wpack[layer, s]).then_inc(s_raw_loaded[s], 16)
                    with sp.Fori(0, UNITS_PAD // RAW_SLOTS - 1) as i:
                        for s in range(RAW_SLOTS):
                            sp.wait_ge(s_split_lo, i * RAW_SLOTS + (s + 1))
                            sp.dma_start(raw[s][:], wpack[layer, i * RAW_SLOTS + (s + RAW_SLOTS)]).then_inc(
                                s_raw_loaded[s], 16)

                @block.gpsimd
                def _(pool):
                    def split(s, nth, n):
                        d = s % SPLIT_SLOTS
                        pool.wait_ge(s_raw_loaded[s], nth * 16)
                        if not isinstance(n, int) or n >= SPLIT_SLOTS:
                            pool.wait_ge(s_unit_used, n - (SPLIT_SLOTS - 1))
                        nc.gpsimd.tensor_tensor(gate_op[:, 0:1], par[:, 0:1], par[:, 0:1], ALU.add)
                        nc.gpsimd.tensor_scalar(w_hi[d][:], raw[s][:], 1.0, 0.0, ALU.mult, ALU.add).then_inc(s_split_hi, 1)
                        pool.wait_ge(s_split_hi, n + 1)
                        nc.gpsimd.tensor_tensor(w_lo[d][:], raw[s][:], w_hi[d][:].bitcast(F32),
                                                ALU.subtract).then_inc(s_split_lo, 1)

                    pool.wait_ge(s_params_loaded, 16)
                    for s in range(RAW_SLOTS):
                        split(s, 1, s)
                    with pool.Fori(1, UNITS_PAD // RAW_SLOTS) as i:
                        for s in range(RAW_SLOTS):
                            split(s, i + 1, i * RAW_SLOTS + s)

                @block.tensor
                def _(pe):
                    unit = [0]

                    def mm(o, l, r, start, stop):
                        return nc.tensor.matmul(o, l, r, start=start, stop=stop, skip_group_check=True)

                    def next_unit():
                        u = unit[0]
                        unit[0] += 1
                        pe.wait_ge(s_split_lo, u + 1)
                        return w_hi[u % SPLIT_SLOTS], w_lo[u % SPLIT_SLOTS]

                    def mm3(o, lh, ll, rh, rl, start, stop):
                        mm(o, lh, rh, start, False)
                        mm(o, lh, rl, False, False)
                        return mm(o, ll, rh, False, stop)

                    def gemm(bank, w, a_hi, a_lo, nk, s0=0, start=True, stop=True, ready=None):
                        for k in range(nk):
                            if ready is not None:
                                ready(k)
                            ins = mm3(bank[:], w[0][:, s0 + k, :], w[1][:, s0 + k, :], a_hi[:, k, :], a_lo[:, k, :],
                                      start and k == 0, stop and k == nk - 1)
                        return ins

                    def gemm_pieces(bank, w, a_hi, a_lo, nk, s0=0, stop=True, signal=None, count=None):
                        for k in range(nk):
                            ins = mm3(bank[:], w[0][:, s0 + k, :], w[1][:, s0 + k, :], a_hi[:, k, :], a_lo[:, k, :],
                                      k == 0, stop and k == nk - 1)
                            if k == nk - 1 and signal is not None:
                                ins.then_inc(signal, 1)
                            yield

                    hcol = lambda h: slice(h * P, h * P + P)
                    tokof = lambda tt: slice(tt * P, tt * P + P)

                    def norm_sum(which):
                        if which:
                            pe.wait_ge(s_ssq, 1)
                        mm(G[6][:], C("ones"), (ssq2 if which else ssq)[:], True, True).then_inc(s_norm_mm, 1)

                    norm_sum(0)

                    def ada_sums(i):
                        pe.wait_ge(s_ada_used, 4 * i + 4)
                        for b in range(4):
                            ins = mm(G[7][:, 16 + 4 * i + b:17 + 4 * i + b], ada_acc[:, i % 2, hcol(b)], C("ones")[:, 0:1],
                                     True, True)
                        ins.then_inc(s_ada_mm, 1)

                    for t in range(16):
                        w = next_unit()
                        if t >= 2:
                            pe.wait_ge(s_conv_raw if t - 2 < 12 else s_z_gated, (t - 1) if t - 2 < 12 else t - 13)
                        rdy = (lambda k: pe.wait_ge(s_h_lo, k + 1)) if t == 0 else None
                        gemm(G[t % 2], w, h_hi, h_lo, KD, ready=rdy).then_inc(s_unit_used, 1)
                        if t in ADA_SUM_AFTER:
                            ada_sums(ADA_SUM_AFTER.index(t))
                    for part in range(4):
                        w = next_unit()
                        for k in (2 * part, 2 * part + 1):
                            b = slice(4 * (k % 2), 4 * (k % 2) + 4)
                            for tt in range(NT):
                                ins = mm3(G[2 + tt][:], h_hi[:, k, tokof(tt)], h_lo[:, k, tokof(tt)],
                                          w[0][:, b, :], w[1][:, b, :], k == 0, k == KD - 1)
                        ins.then_inc(s_unit_used, 1)
                    ada_sums(6)
                    w = next_unit()
                    for k in range(KD):
                        ins = mm3(G[6][0:8, :], w[0][:, k, 0:8], w[1][:, k, 0:8], h_hi[:, k, :], h_lo[:, k, :],
                                  k == 0, k == KD - 1)
                    ins.then_inc(s_unit_used, 1)

                    def mix_work():
                        def head_sum(t):
                            pe.wait_ge(s_dqk_sq, t + 1)
                            if t:
                                pe.wait_ge(s_dqk_r, t)
                            if t == 0:
                                pe.wait_ge(s_dv_out, 4)
                            mix.mark(("sum", t))
                            mm(G[3][:], C("blockones"), sqa[:], True, True).then_inc(s_dqk_mm, 1)

                        for t in range(8):
                            w = next_unit()
                            if t < 2:
                                pe.wait_ge(s_z_gated, 3 + t)
                            if t > 1:
                                pe.wait_ge(s_dqk_out, t - 1)
                            for k, _ in enumerate(gemm_pieces(G[t % 2], w, h_hi, h_lo, KD, signal=s_unit_used)):
                                yield
                                if k == 3 and t:
                                    head_sum(t - 1)
                                    yield
                            mix.made[("qk", t)] = mix.pieces
                        for n in range(KD):
                            w = next_unit()
                            pe.wait_ge(s_dqk_out if n < 2 else s_gate_raw, 7 + n if n < 2 else n - 1)
                            for k, _ in enumerate(gemm_pieces(G[n % 2], w, h_hi, h_lo, KD, signal=s_unit_used)):
                                yield
                                if k == 3 and n == 0:
                                    head_sum(7)
                                    yield
                            mix.made[("gate", n)] = mix.pieces

                    mix_pieces = mix_work()
                    mix.fill(mix_pieces, "ba", 2)
                    pe.wait_ge(s_ba_rows, 1)
                    for tt in range(NT):
                        ins = nc.tensor.transpose(G[6][:, tt * 8:tt * 8 + 8], ba_rows[0:8, tokof(tt)], C("ident")[0:8, 0:8])
                    ins.then_inc(s_ba_tr, 1)
                    ada_sums(7)
                    mix.fill(mix_pieces, "decay", 8)
                    pe.wait_ge(s_dv_out, 4)
                    for t in range(8):
                        pe.wait_ge(s_l2_sq, t + 1)
                        if t > 1:
                            pe.wait_ge(s_l2_r, t - 1)
                        mm(G[4 + t % 2][:], C("ones"), sqg[:, t % 2, :], True, True).then_inc(s_l2_mm, 1)
                        mix.fill(mix_pieces, ("l2", t), 2)
                    pe.wait_ge(s_g_ready, 1)
                    for i, name in enumerate(("tri", "suffix", "first", "second")):
                        ins = mm(G[2][:, 16 * i:16 * i + 16], C(name), gdec, i == 0, i == 3)
                    ins.then_inc(s_gsum_mm, 1)

                    for tt in range(NT):
                        tok = tokof(tt)
                        pe.wait_ge(s_rows_bcast, 2 * tt + 2)
                        pe.wait_ge(s_dec_cols, 1)
                        pe.wait_ge(s_gcol, 1)
                        pe.wait_ge(s_ba_raw, 1)
                        if tt:
                            pe.wait_ge(s_state, 2 * tt + 1)
                            pe.wait_ge(s_vn_made, 2 * tt)
                        for h in range(4):
                            ins = mm(G[2][:, hcol(h)], gb[:, h, :], C("tri"), h == 0, h == 3)
                        ins.then_inc(s_row_mm, 1)
                        for h in range(4):
                            ins = mm(G[6][:, hcol(h)], bb[:, h, :], C("ident"), h == 0, h == 3)
                        ins.then_inc(s_row_mm, 1)
                        pe.wait_ge(s_l2_done, 8)
                        if tt:
                            pe.wait_ge(s_w_out, tt)
                        for h in range(4):
                            ins = mm(G[4][:, hcol(h)], qkv[:, 4 + h, tok], qkv[:, 4 + h, tok], h == 0, h == 3)
                        ins.then_inc(s_kk_mm, 1)
                        for h in range(4):
                            ins = mm(G[5][:, hcol(h)], qkv[:, 4 + h, tok], qkv[:, h, tok], h == 0, h == 3)
                        ins.then_inc(s_kk_mm, 1)
                        mix.fill(mix_pieces, (tt, "rows"), 4)
                        pe.wait_ge(s_at_made, tt + 1)
                        for h in range(4):
                            ins = nc.tensor.transpose(G[5][:, hcol(h)], qkv[:, 8 + h, tok], C("ident"))
                        ins.then_inc(s_vk_tr, 1)
                        pe.wait_ge(s_lt_made, 2 * tt + 1)
                        for h in range(4):
                            ins = nc.tensor.transpose(G[4][:, hcol(h)], qkv[:, 4 + h, tok], C("ident"))
                        ins.then_inc(s_vk_tr, 1)
                        mix.fill(mix_pieces, (tt, "vk"), 3)
                        pe.wait_ge(s_y_made, 6 * tt + 1)
                        pe.wait_ge(s_d_made, 2 * tt + 2)
                        pe.wait_ge(s_eg_made, tt + 1)
                        for h in range(4):
                            ins = nc.tensor.transpose(G[2][:, hcol(h)], Y[:, h, :], C("ident"))
                        ins.then_inc(s_x_tr, 1)
                        mix.fill(mix_pieces, (tt, "x"), 1)
                        for i in range(5):
                            pe.wait_ge(s_bt_made, 5 * tt + i + 1)
                            pe.wait_ge(s_x_made, 5 * tt + i + 1)
                            for h in range(4):
                                ins = mm(G[6][:, hcol(h)], bt[:, h, :], X[:, h, :], h == 0, h == 3)
                            ins.then_inc(s_bx_mm, 1)
                            mix.fill(mix_pieces, (tt, i, 0), 1)
                            pe.wait_ge(s_bx_out, 5 * tt + i + 1)
                            pe.wait_ge(s_kb_made, 2 * tt + 2)
                            pe.wait_ge(s_y_made, 6 * tt + 1 + i)
                            if i < 4:
                                for h in range(4):
                                    ins = mm(G[2][:, hcol(h)], Y[:, h, :], pm[:, h, :], h == 0, h == 3)
                                ins.then_inc(s_yp_mm, 1)
                            for h in range(4):
                                ins = mm(G[4][:, hcol(h)], pm[:, h, :], Y[:, h, :], h == 0, h == 3)
                            ins.then_inc(s_pty_mm, 1)
                            mix.fill(mix_pieces, (tt, i, 1), 1)
                        pe.wait_ge(s_vb_made, tt + 1)
                        pe.wait_ge(s_y_made, 6 * tt + 6)
                        for h in range(4):
                            ins = mm(G[5][:, hcol(h)], kb[:, h, :], Y[:, h, :], h == 0, h == 3)
                        ins.then_inc(s_w_mm, 1)
                        mix.fill(mix_pieces, (tt, "w"), 2)
                        pe.wait_ge(s_w_out, tt + 1)
                        pe.wait_ge(s_qg_made, tt + 1)
                        for c in range(2):
                            n = 2 * tt + c
                            r = slice(64 * c, 64 * c + 64)
                            s_now = S[:, n % 2, :, :]
                            pe.wait_ge(s_state, n + 1)
                            if n:
                                pe.wait_ge(s_vn_made, n)
                            for h in range(4):
                                mm(G[6][r, hcol(h)], Y[:, h, r], vb[:, h, :], h == 0, False)
                                ins = mm(G[6][r, hcol(h)], wt[:, h, r], s_now[:, h, :], False, h == 3)
                            ins.then_inc(s_vn_mm, 1)
                            if c == 0:
                                if tt:
                                    pe.wait_ge(s_o_out, tt)
                            for h in range(4):
                                mm(G[7][:, h * P + 64 * c:h * P + 64 * c + 64], s_now[:, h, :], qg[:, h, r],
                                   h == 0 and c == 0, False)
                            mix.fill(mix_pieces, (tt, "vn", c), 1)
                            pe.wait_ge(s_vn_made, n + 1)
                            for h in range(4):
                                ins = mm(G[2][:, hcol(h)], kd[r, h, :], vn[r, h, :], h == 0, h == 3)
                            ins.then_inc(s_su_mm, 1)
                            for h in range(4):
                                ins = mm(G[7][:, h * P + 64 * c:h * P + 64 * c + 64], vn[r, h, :], at_[r, h, r],
                                         False, h == 3)
                            ins.then_inc(s_o_mm, 1)
                            mix.fill(mix_pieces, (tt, "o", c), 1)
                    def delta_output():
                        for h in range(4):
                            pe.wait_ge(s_on_sq, h + 1)
                            if h > 1:
                                pe.wait_ge(s_on_r, h - 1)
                            mm(G[4 + h % 2][:], C("ones"), sqd[:, h % 2, :], True, True).then_inc(s_on_mm, 1)
                            mix.fill(mix_pieces, ("on", h), 4)
                        mix.fill(mix_pieces, "end", 1000)

                        pe.wait_ge(s_lam_prod, 1)
                        pe.wait_ge(s_vn_made, 8)
                        mm(G[6][:, 0:2], C("ones"), lam_p, True, True).then_inc(s_lam_mm, 1)
                        pe.wait_ge(s_lam_exp, 1)

                    def project(bg, b, banks, hi, lo, o_ready):
                        for n in range(KD):
                            if n % 2 == 0:
                                w = next_unit()
                            if n == 0:
                                pe.wait_ge(o_ready[0], o_ready[1])
                            if n < 2 and b == 0:
                                pe.wait_ge(s_gate_raw, 8)
                            i = b * KD + n
                            if n >= 2 or b:
                                pe.wait_ge(s_gate_merge, i - 1)
                            if n < 2 and b == 1:
                                pe.wait_ge(s_mqk_rope, 8)
                                pe.wait_ge(s_mqk_r, 8)
                            yield from gemm_pieces(banks[n % 2], w, hi, lo, 4, s0=4 * (n % 2),
                                                   signal=s_unit_used if n % 2 else s_proj_even)
                            bg.made[("proj", b, n)] = bg.pieces

                    def diff_work():
                        yield from project(diff, 0, (G[0], G[1]), o_hi, o_lo, (s_branch_o, 4))

                        def lat_sum(t):
                            pe.wait_ge(s_lat_sq, t + 1)
                            if t == 0:
                                pe.wait_ge(s_on_r, 4)
                            diff.mark(("latsum", t))
                            mm(G[4 if t < 3 else 5][:], C("ones"), sqm[:, t % 2, :], t in (0, 3), t in (2, 4)).then_inc(s_lat_mm, 1)

                        for t in range(6):
                            w = next_unit()
                            pe.wait_ge(s_gate_merge if t < 2 else s_lat_out, 7 + t if t < 2 else t - 1)
                            yield from gemm_pieces(G[t % 2], w, h_hi, h_lo, KD, signal=s_unit_used)
                            diff.made[("lat", t)] = diff.pieces
                            if t:
                                lat_sum(t - 1)
                                yield

                        def head_sum(t):
                            pe.wait_ge(s_mqk_sq, t + 1)
                            if t:
                                pe.wait_ge(s_mqk_r, t)
                            if t == 0:
                                pe.wait_ge(s_lat_r, 2)
                            diff.mark(("sum", t))
                            mm(G[4][:], C("ones"), sqm[:, t % 2, :], True, True).then_inc(s_mqk_ss, 1)

                        def head_rot(t):
                            pe.wait_ge(s_mqk_y, t + 1)
                            if t:
                                pe.wait_ge(s_mqk_rope, t)
                            diff.mark(("rot", t))
                            mm(G[5][:], C("rot"), my[:, t % 2, :], True, True).then_inc(s_mqk_rot, 1)

                        for t in range(8):
                            if t in (0, 2, 4):
                                w = next_unit()
                            if t < 2:
                                pe.wait_ge(s_lat_out, 5 + t)
                            if t > 1:
                                pe.wait_ge(s_mqk_y, t - 1)
                            pe.wait_ge(s_lat_lo, 3 if t < 4 else 5)
                            last = s_unit_used if t in MQK_LAST else s_mqk_mm
                            if t < 4:
                                pieces = gemm_pieces(G[t % 2], w, lat_hi, lat_lo, 3, s0=3 * (t % 2), signal=last)
                            else:
                                pieces = gemm_pieces(G[t % 2], w, lat_hi[:, 3:5, :], lat_lo[:, 3:5, :], 2, s0=2 * (t - 4),
                                                     stop=False)
                            for k, _ in enumerate(pieces):
                                yield
                                if k == 0 and t:
                                    head_sum(t - 1)
                                    yield
                            if t >= 4:
                                mm(G[t % 2][:], C("ident"), lat[:, 5, :], False, True).then_inc(last, 1)
                                yield
                            diff.made[("head", t)] = diff.pieces
                            if t >= 2:
                                head_rot(t - 2)
                                yield
                        w = next_unit()

                        def latent_v(tt):
                            for k in range(2):
                                ins = mm3(G[tt % 2][:], lat_hi[:, 3 + k, tokof(tt)], lat_lo[:, 3 + k, tokof(tt)],
                                          w[0][:, 4 * k:4 * k + 4, :], w[1][:, 4 * k:4 * k + 4, :], k == 0, k == 1)
                                if k == 1:
                                    ins.then_inc(s_unit_used if tt == NT - 1 else s_mv_mm, 1)
                                yield
                            diff.made[("v", tt)] = diff.pieces

                        pe.wait_ge(s_mqk_y, 7)
                        yield from latent_v(0)
                        head_sum(7)
                        yield
                        head_rot(6)
                        yield
                        for _ in range(6):
                            yield
                        pe.wait_ge(s_mqk_y, 8)
                        yield from latent_v(1)
                        head_rot(7)
                        yield
                        for tt in (2, 3):
                            pe.wait_ge(s_mv_out, tt - 1)
                            yield from latent_v(tt)

                    def attention(bg, work, maps, fills, rows, qs, ks, vs, prob, ptile, tag, first, between):
                        items = [(h, qb) for h in range(4) for qb in range(NT)]

                        def scores(i):
                            h, qb = items[i]
                            nk = (qb + 1) * P
                            for m in range(maps):
                                bank = G[2 + m] if maps == 2 else G[2 + i % 2]
                                if (maps * (i - 1) + m + 1 if maps == 2 else i - 1) > 0:
                                    pe.wait_ge(tag["exp"], maps * (i - 1) + m + 1 if maps == 2 else i - 1)
                                mm(bank[:, 0:nk], qs(h)[rows[m], qb * P:qb * P + P], ks(h)[rows[m], 0:nk], True, False)
                                ins = mm(bank[:, nk - 64:nk], mask_row[0:1, 0:P], mask_row[0:1, P:P + CHUNK], False, True)
                                ins.then_inc(tag["qk"], 1)

                        first()
                        scores(0)
                        between()
                        for i, (h, qb) in enumerate(items):
                            bg.fill(work, (i, 0), fills[0])
                            if i + 1 < len(items):
                                scores(i + 1)
                            bg.fill(work, (i, 1), fills[1])
                            pe.wait_ge(tag["p"], i + 1)
                            if i:
                                pe.wait_ge(tag["pt"], i)
                            for b in range(qb + 1):
                                ins = nc.tensor.transpose(G[6][:, b * P:b * P + P], prob(i)[:, b * P:b * P + P], C("ident"))
                            ins.then_inc(tag["tr"], 1)
                            bg.fill(work, (i, 2), fills[2])
                            pe.wait_ge(tag["pt"], i + 1)
                            if qb == 0:
                                if h:
                                    pe.wait_ge(tag["o"], h)
                            for b in range(qb + 1):
                                ins = mm(G[7][:, qb * P:qb * P + P], vs(b, h), ptile(i)[:, b, :],
                                         b == 0 and qb == 0, b == qb)
                            ins.then_inc(tag["pv"], 1)

                    def diff_first():
                        pe.wait_ge(s_mask_made, 1)
                        pe.wait_ge(s_state, 9)
                        pe.wait_ge(s_dqk_r, 8)
                        pe.wait_ge(s_o_out, 4)

                    work = diff_work()
                    attention(diff, work, 2, (4, 2, 3), (slice(0, 64), slice(64, 128)),
                              lambda h: dqkv[:, h, :], lambda h: dqkv[:, 4 + h, :], lambda b, h: dqkv[:, 8 + b, hcol(h)],
                              lambda i: probs[:, i % 2, 0, :], lambda i: pt[:, i % 2], f_da, diff_first, delta_output)
                    diff.fill(work, "end", 1000)
                    def mla_work():
                        for b in range(2):
                            for n in range(KD):
                                w = next_unit()
                                if n < 2 and b == 0:
                                    pe.wait_ge(s_mv_out, 3 + n)
                                if b * KD + n - 1 > 0:
                                    pe.wait_ge(s_gate2_tanh, b * KD + n - 1)
                                yield from gemm_pieces(G[n % 2], w, h_hi, h_lo, KD, signal=s_unit_used)
                                mla.made[("gate", b, n)] = mla.pieces
                            if b == 0:
                                pe.wait_ge(s_sub_r, 4)
                                yield from project(mla, 1, (G[4], G[5]), o_hi, o_lo, (s_branch_o, 8))

                    work = mla_work()
                    def diff_output():
                        for h in range(4):
                            pe.wait_ge(s_sub_sq, h + 1)
                            if h > 1:
                                pe.wait_ge(s_sub_r, h - 1)
                            if h < 2:
                                pe.wait_ge(s_mqk_r, 8)
                                pe.wait_ge(s_mqk_rope, 8)
                            mm(G[4 + h % 2][:], C("ones"), sqo[:, h % 2, :], True, True).then_inc(s_sub_mm, 1)
                            mla.fill(work, ("sub", h), SUB_FILL[h])

                    attention(mla, work, 1, (3, 2, 3), (slice(0, 128),),
                              lambda h: mq[:, h, :], lambda h: mq[:, 4 + h, :],
                              lambda b, h: mv[:, b, hcol(h)],
                              lambda i: mprobs[:, i % 2, :], lambda i: mpt[:, i % 2], f_ma, lambda: pe.wait_ge(s_da_o, 4), diff_output)
                    mla.fill(work, "end", 1000)
                    for _ in project(mla, 2, (G[4], G[5]), ob_hi, ob_lo, (s_ma_o, 4)):
                        pass

                    for n in range(KD):
                        w = next_unit()
                        if n < 2:
                            pe.wait_ge(s_gate2_tanh, 2 * KD)
                        if n > 1:
                            pe.wait_ge(s_x_mid, n - 1)
                        rdy = (lambda k: pe.wait_ge(s_m_lo, k + 1)) if n == 0 else None
                        gemm(G[n % 2], w, m_hi, m_lo, KD, ready=rdy).then_inc(s_unit_used, 1)
                    norm_sum(1)

                    def gate_up(j, e, first_block):
                        for half in range(2):
                            s = (U_GU + half) % SPLIT_SLOTS
                            pe.wait_ge(s_split_lo, j * 2 + (U_GU + half + 1))
                            if not first_block:
                                pe.wait_ge(s_ffn_y2 if half else s_ffn_y, j - 1)
                            rdy = (lambda k: pe.wait_ge(s_h_lo, 8 + k + 1)) if first_block and e == 0 and half == 0 else None
                            gemm(G[2 * half + e], (w_hi[s], w_lo[s]), h_hi, h_lo, KD, ready=rdy).then_inc(s_unit_used, 1)

                    pe.wait_ge(s_x_mid, 8)
                    pe.wait_ge(s_ma_exp, 16)
                    gate_up(0, 0, True)
                    gate_up(1, 1, True)
                    with pe.Fori(1, KF // 2) as i:
                        gate_up(i * 2, 0, False)
                        gate_up(i * 2 + 1, 1, False)

                    def down(n, e, first_block):
                        if not first_block:
                            pe.wait_ge(s_x_new, n - 1)
                        for part, nk in enumerate((8, 8, 6)):
                            c = 3 * e + part
                            s = (U_DOWN + c) % SPLIT_SLOTS
                            pe.wait_ge(s_split_lo, n * 3 + (U_DOWN + part + 1))
                            k0 = 8 * part
                            rdy = (lambda k: pe.wait_ge(s_ffn_lo, min(k0 + k + 1, KF))) if first_block and e == 0 else None
                            gemm(G[e], (w_hi[s], w_lo[s]), hid_hi[:, k0:k0 + nk, :], hid_lo[:, k0:k0 + nk, :], nk,
                                 start=part == 0, stop=part == 2, ready=rdy).then_inc(s_unit_used, 1)

                    def next_ada_sums(i):
                        pe.wait_ge(s_ada2_step, i * 8 + 8)
                        if not isinstance(i, int):
                            pe.wait_ge(s_mod_next, i)
                        for b in range(4):
                            ins = mm(G[7][:, b:b + 1], ada_acc2[:, hcol(b)], C("ones")[:, 0:1], True, True)
                        ins.then_inc(s_ada2_mm, 1)

                    pe.wait_ge(s_ffn_y, KF)
                    down(0, 0, True)
                    down(1, 1, True)
                    next_ada_sums(0)
                    with pe.Fori(1, KD // 2) as i:
                        down(i * 2, 0, False)
                        down(i * 2 + 1, 1, False)
                        next_ada_sums(i)

                @block.scalar
                def _(act):
                    A = nc.scalar.activation
                    s_chain = s_scalar_step
                    chain = [0]

                    def link(ins):
                        chain[0] += 1
                        ins.then_inc(s_chain, 1)
                        act.wait_ge(s_chain, chain[0])


                    def norm(which):
                        act.wait_ge(s_norm_mm, which + 1)
                        rstd(rn[:], G[6][:], 1.0 / D, s_norm_r)
                        if which == 0:
                            for n in range(ADA1_SLOTS):
                                load_ada(n)
                            act.wait_ge(s_params_loaded, 16)
                        act.wait_ge(s_mod_ready, 1)
                        for k in range(KD):
                            act.wait_ge(s_norm_t, which * KD + k + 1)
                            c = 3 * which * KD + k
                            A(h_hi[:, k, :], tn[:, k % 2, :], ACT.Identity, bias=mod[:, c:c + 1]).then_inc(s_h_hi, 1)

                    def rstd(dst, src, scale, s_made, out_bias=0.0):
                        link(A(dst, src, ACT.Ln, scale=scale, bias=eps))
                        A(dst, dst, ACT.Exp, scale=-0.5, bias=out_bias).then_inc(s_made, 1)

                    def load_ada(n):
                        s = n % ADA1_SLOTS
                        if n - ADA1_SLOTS + 1 > 0:
                            act.wait_ge(s_ada_used, n - ADA1_SLOTS + 1)
                        act.dma_start(ada1[s][:], apack[layer, n]).then_inc(s_ada1_loaded[s], 16)

                    norm(0)
                    act.wait_ge(s_norm_t, KD)
                    act.dma_start(x_spill, x[:]).then_inc(s_x_spilled, 16)

                    act.preload_act_table_set("exp_and_others")

                    def conv_tanh(t):
                        act.wait_ge(s_conv_y, t + 1)
                        if t > 1:
                            act.wait_ge(s_conv_out, t - 1)
                        A(ct[:, t % 2, :], cy[:, t % 2, :], ACT.Tanh, scale=0.5).then_inc(s_conv_tanh, 1)

                    loaded = ADA1_SLOTS

                    def load_upto(n):
                        nonlocal loaded
                        while loaded < n:
                            load_ada(loaded)
                            loaded += 1

                    for t in range(12):
                        act.wait_ge(s_unit_used, U_CONV + t + 1)
                        if t > 1:
                            act.wait_ge(s_conv_y, t - 1)
                        act.wait_ge(s_craw_zero, 1)
                        A(craw[:, t % 2, 3:], G[t % 2][:], ACT.Copy).then_inc(s_conv_raw, 1)
                        if t:
                            conv_tanh(t - 1)
                        act.wait_ge(s_conv_raw, t + 1)
                        if t > 1:
                            act.wait_ge(s_conv_out, t - 1)
                        A(cy[:, t % 2, :], craw[:, t % 2, 0:T], ACT.Copy, scale=PAR("conv", 4 * t)).then_inc(s_conv_y0, 1)
                        load_upto(3 * t // 2 + ADA1_SLOTS - 2)
                    conv_tanh(11)
                    for t in range(12, 16):
                        act.wait_ge(s_unit_used, U_CONV + t + 1)
                        act.wait_ge(s_conv_out if t < 14 else s_z_gated, t - 1 if t < 14 else t - 13)
                        A(ct[:, t % 2, :], G[t % 2][:], ACT.Tanh, scale=0.5).then_inc(s_z_tanh, 1)
                        load_upto(2 * t + ADA1_SLOTS - 7)
                    load_upto(4 * ADA_REST - 2)
                    act.wait_ge(s_unit_used, U_DV + 4)
                    for tt in range(NT):
                        A(dqkv[:, 8 + tt, :], G[2 + tt][:], ACT.Copy).then_inc(s_dv_out, 1)
                    load_upto(4 * ADA_REST)
                    act.wait_ge(s_unit_used, U_BA + 1)
                    A(ba_rows[0:8, :], G[6][0:8, :], ACT.Copy).then_inc(s_ba_rows, 1)
                    act.wait_ge(s_ba_tr, 1)
                    A(ba, G[6][:, 0:32], ACT.Copy).then_inc(s_ba_raw, 1)
                    act.wait_ge(s_ba_raw, 1)
                    bav = ba.rearrange("p (t c) -> p t c", c=8)
                    A(beta.rearrange("p (t c) -> p t c", c=4), bav[:, :, 0:4], ACT.Tanh, scale=0.5).then_inc(s_beta_tanh, 1)
                    act.preload_act_table_set("natural_log_exp_and_others")
                    A(ealog, PAR("a_log", 0, 16), ACT.Exp).then_inc(s_alog_exp, 1)
                    act.wait_ge(s_sp_abs, 1)
                    link(A(sp_abs, sp_abs, ACT.Exp, scale=-1.0))
                    A(sp_abs, sp_abs, ACT.Ln, bias=1.0).then_inc(s_sp_ln, 1)

                    def mix_work():
                        for t in range(8):
                            if t:
                                yield mix.made[("sum", t - 1)]
                                act.wait_ge(s_dqk_mm, t)
                                if t > 1:
                                    act.wait_ge(s_dqk_out, t - 1)
                                rstd(ra[:], G[3][:], 1.0 / QK, s_dqk_r)
                            yield mix.made[("qk", t)]
                            act.wait_ge(s_unit_used, U_DIFF + t + 1)
                            A(sqa[:], G[t % 2][:], ACT.Square).then_inc(s_dqk_sq, 1)
                        yield mix.made[("sum", 7)]
                        act.wait_ge(s_dqk_mm, 8)
                        act.wait_ge(s_dqk_out, 7)
                        rstd(ra[:], G[3][:], 1.0 / QK, s_dqk_r)
                        for n in range(KD):
                            yield mix.made[("gate", n)]
                            act.wait_ge(s_unit_used, U_GATE_C + n + 1)
                            A(gates[:, n, :], G[n % 2][:], ACT.Copy).then_inc(s_gate_raw, 1)

                    bg = mix_bg = Follower(mix, mix_work())
                    bg.upto("ba")
                    act.wait_ge(s_ada_used, 4 * ADA_REST)
                    act.wait_ge(s_ada_mm, ADA_REST)
                    for t in range(8):
                        act.wait_ge(s_conv_out, t + 1)
                        if t > 1:
                            act.wait_ge(s_l2_mm, t - 1)
                        A(sqg[:, t % 2, :], qkv[:, t, :], ACT.Square).then_inc(s_l2_sq, 1)
                        if t == 1:
                            bg.upto("decay")
                        if t:
                            act.wait_ge(s_l2_mm, t)
                            if t > 2:
                                act.wait_ge(s_l2_done, t - 2)
                            rstd(rg[:, (t - 1) % 2, :], G[4 + (t - 1) % 2][:], 0.25, s_l2_r,
                                 out_bias=ln_half_q if t - 1 < 4 else ln_half)
                            bg.upto(("l2", t - 1))
                    act.wait_ge(s_l2_mm, 8)
                    act.wait_ge(s_l2_done, 6)
                    rstd(rg[:, 1, :], G[5][:], 0.25, s_l2_r, out_bias=ln_half)
                    act.wait_ge(s_gsum_mm, 1)
                    A(gcol, G[2][:, 0:16], ACT.Copy).then_inc(s_gcol, 1)
                    A(dec, G[2][:, 0:64], ACT.Exp).then_inc(s_dec_cols, 1)
                    bg.upto(("l2", 7))
                    H4 = lambda ap: ap.rearrange("p (h t) -> p h t", h=4)
                    for tt in range(NT):
                        act.wait_ge(s_row_mm, 2 * tt + 1)
                        act.wait_ge(s_d_made, 2 * tt + 1)
                        A(eg[:], H4(G[2][:]), ACT.Exp).then_inc(s_eg_made, 1)
                        act.wait_ge(s_d_made, 2 * tt + 2)
                        A(dt_[:], dt_[:], ACT.Exp).then_inc(s_dt_exp, 1)
                        bg.upto((tt, "rows"))
                        bg.upto((tt, "vk"))
                        bg.upto((tt, "x"))
                        for i in range(5):
                            act.wait_ge(s_bx_mm, 5 * tt + i + 1)
                            if i:
                                act.wait_ge(s_pty_mm, 5 * tt + i)
                            A(pm[:], H4(G[6][:]), ACT.Copy).then_inc(s_bx_out, 1)
                            bg.upto((tt, i, 0))
                            bg.upto((tt, i, 1))
                        act.wait_ge(s_w_mm, tt + 1)
                        A(wt[:], H4(G[5][:]), ACT.Copy, scale=-1.0).then_inc(s_w_out, 1)
                        bg.upto((tt, "w"))
                        for c in range(2):
                            r = slice(64 * c, 64 * c + 64)
                            act.wait_ge(s_vn_mm, 2 * tt + c + 1)
                            if 2 * (tt - 1) + c + 1 > 0:
                                act.wait_ge(s_o_mm, 2 * (tt - 1) + c + 1)
                            A(vn[r], H4(G[6][r, :]), ACT.Copy).then_inc(s_vn_made, 1)
                            if c:
                                act.wait_ge(s_o_mm, 2 * tt + 2)
                                A(qkv[:, 8:12, tt * P:tt * P + P], H4(G[7][:]), ACT.Copy).then_inc(s_o_out, 1)
                            bg.upto((tt, "vn", c))
                            bg.upto((tt, "o", c))
                    def delta_output():
                        act.wait_ge(s_o_out, 4)
                        for h in range(5):
                            if h < 4:
                                if h > 1:
                                    act.wait_ge(s_on_mm, h - 1)
                                A(sqd[:, h % 2, :], qkv[:, 8 + h, :], ACT.Square).then_inc(s_on_sq, 1)
                            if h:
                                g = h - 1
                                act.wait_ge(s_on_mm, g + 1)
                                if g > 1:
                                    act.wait_ge(s_on_y, g - 1)
                                rstd(rd[:, g % 2, :], G[4 + g % 2][:], 1.0 / P, s_on_r, out_bias=ln_half)
                                mix_bg.upto(("on", g))
                        mix_bg.finish()

                        act.preload_act_table_set("exp_and_others")
                        act.wait_ge(s_lam_mm, 1)
                        A(lam_e, G[6][:, 0:2], ACT.Exp).then_inc(s_lam_exp, 1)

                    def attention(bg, maps, prob, ptile, tag, scale, between):
                        def exps(i):
                            nk = (i % 4 + 1) * P
                            for m in range(maps):
                                act.wait_ge(tag["nm"], i + 1)
                                if m == 0:
                                    if i > 1:
                                        act.wait_ge(tag["tr"], i - 1)
                                c = maps * (i % 2) + m
                                bank = G[2 + m] if maps == 2 else G[2 + i % 2]
                                A(prob(i, m)[:, 0:nk], bank[:, 0:nk], ACT.Exp, scale=scale,
                                  bias=nm[:, c:c + 1], accum_out=rs[:, c:c + 1]).then_inc(tag["exp"], 1)

                        exps(0)
                        between()
                        for i in range(16):
                            bg.upto((i, 0))
                            if i + 1 < 16:
                                exps(i + 1)
                            nb = i % 4 + 1
                            act.wait_ge(tag["tr"], i + 1)
                            if i > 1:
                                act.wait_ge(tag["pv"], i - 1)
                            A(ptile(i)[:, 0:nb, :], G[6][:, 0:nb * P].rearrange("p (b t) -> p b t", b=nb), ACT.Copy).then_inc(tag["pt"], 1)
                            bg.upto((i, 1))
                            bg.upto((i, 2))

                    def diff_work():
                        for n in range(0, KD, 2):
                            yield 3 * n // 2 + 1
                            act.wait_ge(s_gate_raw, n + 2)
                            A(gates[:, n:n + 2, :], gates[:, n:n + 2, :], ACT.Tanh, scale=0.5).then_inc(s_gate_tanh, 1)
                        yield diff.made[("proj", 0, KD - 1)]
                        act.preload_act_table_set("natural_log_exp_and_others")
                        for t in range(6):
                            yield diff.made[("lat", t)]
                            act.wait_ge(s_unit_used, U_LAT + t + 1)
                            if t < 5:
                                if t > 1:
                                    act.wait_ge(s_lat_mm, t - 1)
                                A(sqm[:, t % 2, :], G[t % 2][:], ACT.Square).then_inc(s_lat_sq, 1)
                            A(lat[:, t, :], G[t % 2][:], ACT.Copy).then_inc(s_lat_out, 1)
                            if t in (3, 5):
                                yield diff.made[("latsum", 2 if t == 3 else 4)]
                                act.wait_ge(s_lat_mm, 3 if t == 3 else 5)
                                rstd(rm[:, t // 5, :], G[4 + t // 5][:], 1.0 / (384 if t == 3 else 256), s_lat_r)
                        for t in range(8):
                            if t:
                                yield diff.made[("sum", t - 1)]
                                act.wait_ge(s_mqk_ss, t)
                                if t > 2:
                                    act.wait_ge(s_mqk_y, t - 2)
                                rstd(rm[:, (t - 1) % 2, :], G[4][:], 1.0 / MQK, s_mqk_r)
                            yield diff.made[("head", t)]
                            if t in MQK_LAST:
                                act.wait_ge(s_unit_used, U_QUP + MQK_LAST.index(t) + 1)
                            else:
                                act.wait_ge(s_mqk_mm, t + 1 - sum(i < t for i in MQK_LAST))
                            if t > 1:
                                act.wait_ge(s_mqk_ss, t - 1)
                            A(sqm[:, t % 2, :], G[t % 2][:], ACT.Square).then_inc(s_mqk_sq, 1)
                        yield diff.made[("sum", 7)]
                        act.wait_ge(s_mqk_ss, 8)
                        act.wait_ge(s_mqk_y, 6)
                        rstd(rm[:, 1, :], G[4][:], 1.0 / MQK, s_mqk_r)
                        for tt in range(NT):
                            yield diff.made[("v", tt)]
                            if tt == NT - 1:
                                act.wait_ge(s_unit_used, U_VUP + 1)
                            else:
                                act.wait_ge(s_mv_mm, tt + 1)
                            A(mv[:, tt, :], G[tt % 2][:], ACT.Copy).then_inc(s_mv_out, 1)

                    bg = Follower(diff, diff_work())
                    attention(bg, 2, lambda i, m: probs[:, i % 2, m, :], lambda i: pt[:, i % 2], f_da, QK ** -0.5, delta_output)
                    bg.finish()
                    def diff_output():
                        for h in range(5):
                            if h < 4:
                                act.wait_ge(s_da_o, h + 1)
                                if h > 1:
                                    act.wait_ge(s_sub_mm, h - 1)
                                A(sqo[:, h % 2, :], oraw[:, h, :], ACT.Square).then_inc(s_sub_sq, 1)
                            if h:
                                g = h - 1
                                act.wait_ge(s_sub_mm, g + 1)
                                if g > 1:
                                    act.wait_ge(s_sub_y, g - 1)
                                rstd(ro[:, g % 2, :], G[4 + g % 2][:], 1.0 / P, s_sub_r)
                        act.preload_act_table_set("exp_and_others")

                    def mla_work():
                        for b in range(2):
                            for n in range(KD):
                                yield mla.made[("gate", b, n)]
                                act.wait_ge(s_unit_used, (U_GATE_B if b else U_GATE_A) + n + 1)
                                if b and n == 0:
                                    act.wait_ge(s_gate_merge, 2 * KD)
                                A(gates2[:, n, :], G[n % 2][:], ACT.Tanh, scale=0.5).then_inc(s_gate2_tanh, 1)

                    bg = Follower(mla, mla_work())
                    attention(bg, 1, lambda i, m: mprobs[:, i % 2, :], lambda i: mpt[:, i % 2], f_ma, MQK ** -0.5, diff_output)
                    bg.finish()
                    act.wait_ge(s_unit_used, U_PROJ_A + 4)
                    act.dma_start(x[:], x_spill).then_inc(s_x_back, 16)
                    act.preload_act_table_set("natural_log_exp_and_others")
                    norm(1)
                    act.preload_act_table_set("exp_and_others")
                    act.wait_ge(s_unit_used, U_OUT + 8)
                    for s in range(ADA_SLOTS):
                        act.dma_start(ada2[s][:], apack[layer, 4 * ADA_REST + s]).then_inc(s_ada2_loaded[s], 16)

                    def ffn_tanh(j, e, first_block):
                        act.wait_ge(s_unit_used, j * 2 + (U_GU + 1))
                        if not first_block:
                            act.wait_ge(s_ffn_y, j - 1)
                        A(ft[:, e, :], G[e][:], ACT.Tanh, scale=0.5).then_inc(s_ffn_tanh, 1)

                    ffn_tanh(0, 0, True)
                    ffn_tanh(1, 1, True)
                    with act.Fori(1, KF // 2) as i:
                        ffn_tanh(i * 2, 0, False)
                        ffn_tanh(i * 2 + 1, 1, False)
                    with act.Fori(0, ADA_FIRST - 1) as i:
                        for s in range(ADA_SLOTS):
                            act.wait_ge(s_ada2_step, i * 8 + (2 * s + 2))
                            act.dma_start(ada2[s][:], apack[layer, i * 4 + (4 * ADA_REST + 4 + s)]).then_inc(
                                s_ada2_loaded[s], 16)
                    act.preload_act_table_set("natural_log_exp_and_others")

                @block.vector
                def _(dve):
                    V = nc.vector
                    chain = [0]
                    s_chain = s_vector_step

                    def link(ins):
                        chain[0] += 1
                        ins.then_inc(s_chain, 1)
                        dve.wait_ge(s_chain, chain[0])


                    def hd(ap):
                        return ap.rearrange("p (h t) -> p h t", h=4)

                    dve.wait_ge(s_params_loaded, 16)
                    V.tensor_tensor(mod[:, 0:16], mod_raw[:, 0:16], PAR("ada_b", 0, 16), ALU.add).then_inc(s_mod_ready, 1)
                    dve.wait_ge(s_mod_ready, 1)
                    link(V.scalar_tensor_tensor(out=normA[:, 0, :], in0=mod[:, KD:2 * KD], scalar=1.0, in1=PAR("norm1", 0, 8),
                                                op0=ALU.add, op1=ALU.mult))

                    def norm(which):
                        def lo(k):
                            dve.wait_ge(s_h_hi, which * KD + k + 1)
                            c = 3 * which * KD + k
                            V.scalar_tensor_tensor(out=h_lo[:, k, :], in0=tn[:, k % 2, :], scalar=mod[:, c:c + 1],
                                                   in1=h_hi[:, k, :].bitcast(F32), op0=ALU.add, op1=ALU.subtract).then_inc(s_h_lo, 1)
                        dve.wait_ge(s_norm_r, which + 1)
                        for k in range(KD):
                            if k >= 2:
                                dve.wait_ge(s_h_lo, which * KD + k - 1)
                            V.scalar_tensor_tensor(out=tn[:, k % 2, :], in0=x[:, k, :], scalar=normA[:, which, k:k + 1],
                                                   in1=rn[:], op0=ALU.mult, op1=ALU.mult).then_inc(s_norm_t, 1)
                            if k:
                                lo(k - 1)
                        lo(KD - 1)

                    norm(0)
                    lp = PAR("lambda", 0, 4).rearrange("p (a b) -> p a b", b=2)
                    V.tensor_tensor(lam_p, lp[:, :, 0], lp[:, :, 1], ALU.mult).then_inc(s_lam_prod, 1)
                    link(V.tensor_tensor(subw, PAR("subln"), PAR("one_minus_init"), ALU.mult))

                    def ada_steps():
                        for g in range(ADA_REST):
                            acc = ada_acc[:, g % 2, :]
                            for k in range(KD):
                                m = 4 * g + k // 2
                                if k == 0:
                                    if g > 1:
                                        dve.wait_ge(s_ada_mm, g - 1)
                                dve.wait_ge(s_ada1_loaded[m % ADA1_SLOTS], 16 * (m // ADA1_SLOTS + 1))
                                part = ada1[m % ADA1_SLOTS][:, k % 2, :]
                                if k == 0:
                                    link(V.tensor_scalar(acc, part, c_col[:, 0:1], None, ALU.mult))
                                elif k % 2 == 0:
                                    link(V.scalar_tensor_tensor(out=acc, in0=part, scalar=c_col[:, k:k + 1], in1=acc,
                                                                op0=ALU.mult, op1=ALU.add))
                                else:
                                    V.scalar_tensor_tensor(out=acc, in0=part, scalar=c_col[:, k:k + 1], in1=acc,
                                                           op0=ALU.mult, op1=ALU.add).then_inc(s_ada_used, 1)
                                    dve.wait_ge(s_ada_used, m + 1)
                                yield

                    ada = ada_steps()

                    V.memset(craw[:, :, 0:3], 0.0).then_inc(s_craw_zero, 1)

                    def silu(t):
                        dve.wait_ge(s_conv_tanh, t + 1)
                        V.scalar_tensor_tensor(out=qkv[:, t, :], in0=ct[:, t % 2, :], scalar=1.0, in1=cy[:, t % 2, :],
                                               op0=ALU.add, op1=ALU.mult).then_inc(s_conv_out, 1)
                    for t in range(12):
                        dve.wait_ge(s_conv_y0, t + 1)
                        y = cy[:, t % 2, :]
                        for i in range(1, 4):
                            ins = V.scalar_tensor_tensor(out=y, in0=craw[:, t % 2, i:i + T], scalar=PAR("conv", 4 * t + i),
                                                         in1=y, op0=ALU.mult, op1=ALU.add)
                            if i < 3:
                                link(ins)
                        ins.then_inc(s_conv_y, 1)
                        for _ in range(2):
                            next(ada, None)
                        if t:
                            silu(t - 1)
                        next(ada, None)
                    silu(11)
                    for t in range(12, 16):
                        dve.wait_ge(s_z_tanh, t - 11)
                        V.scalar_tensor_tensor(out=z_t[:, t - 12, :], in0=ct[:, t % 2, :], scalar=1.0, in1=G[t % 2][:],
                                               op0=ALU.add, op1=ALU.mult).then_inc(s_z_gated, 1)
                        for _ in range(4):
                            next(ada, None)
                    for _ in ada:
                        pass
                    dve.wait_ge(s_ba_raw, 1)
                    av = ba.rearrange("p (t c) -> p t c", c=8)[:, :, 4:8]
                    r4 = lambda ap: ap.rearrange("p (t c) -> p t c", c=4)
                    link(V.tensor_tensor(r4(gdec), av, r4(PAR("dt_bias", 0, 16)), ALU.add))
                    link(V.tensor_scalar(sp_relu, gdec, -1.0, None, ALU.mult))
                    link(V.tensor_tensor(sp_abs, gdec, sp_relu, ALU.max))
                    V.tensor_scalar(sp_relu, gdec, 0.0, None, ALU.max).then_inc(s_sp_abs, 1)
                    dve.wait_ge(s_beta_tanh, 1)
                    link(V.tensor_scalar(beta, beta, 0.5, 0.5, ALU.mult, ALU.add))
                    link(V.tensor_scalar(beta_half, beta, 0.5, None, ALU.mult))
                    dve.wait_ge(s_sp_ln, 1)
                    dve.wait_ge(s_alog_exp, 1)
                    link(V.tensor_tensor(sp_relu, sp_relu, sp_abs, ALU.add))
                    V.scalar_tensor_tensor(out=gdec, in0=sp_relu, scalar=-1.0, in1=ealog, op0=ALU.mult, op1=ALU.mult).then_inc(s_g_ready, 1)
                    dve.wait_ge(s_ada_mm, ADA_REST)
                    link(V.tensor_tensor(mod[:, 16:48], G[7][:, 16:48], PAR("ada_b", 16, 32), ALU.add))
                    V.tensor_scalar(half_g[:, 0, :], mod[:, 2 * KD:3 * KD], 0.5, None, ALU.mult)
                    V.tensor_scalar(half_g[:, 1, :], mod[:, 5 * KD:6 * KD], 0.5, None, ALU.mult)
                    link(V.scalar_tensor_tensor(out=normA[:, 1, :], in0=mod[:, 4 * KD:5 * KD], scalar=1.0, in1=PAR("norm2", 0, 8),
                                                op0=ALU.add, op1=ALU.mult))

                    def mix_work():
                        for t in range(8):
                            yield mix.made[("sum", t)]
                            dve.wait_ge(s_dqk_r, t + 1)
                            V.scalar_tensor_tensor(out=dqkv[:, t, :], in0=G[t % 2][:], scalar=PAR("diff_q" if t < 4 else "diff_k"),
                                                   in1=ra[:], op0=ALU.mult, op1=ALU.mult).then_inc(s_dqk_out, 1)

                    bg = mix_bg = Follower(mix, mix_work())
                    bg.upto("decay")
                    for t in range(8):
                        dve.wait_ge(s_l2_r, t + 1)
                        V.tensor_tensor(qkv[:, t, :], qkv[:, t, :], rg[:, t % 2, :], ALU.mult).then_inc(s_l2_done, 1)
                        bg.upto(("l2", t))
                    dve.wait_ge(s_dec_cols, 1)
                    dve.wait_ge(s_gcol, 1)
                    dve.wait_ge(s_g_ready, 1)
                    link(V.tensor_tensor(beta_eg, beta, e_g, ALU.mult))
                    V.memset(S[:, 0], 0.0).then_inc(s_state, 1)
                    for tt in range(NT):
                        tc = slice(4 * tt, 4 * tt + 4)
                        tok = slice(tt * P, tt * P + P)
                        if tt:
                            dve.wait_ge(s_row_mm, 2 * tt)
                        if tt:
                            dve.wait_ge(s_qg_made, tt)
                        V.tensor_copy(gb[:], group(gdec[:, tc], P)).then_inc(s_rows_bcast, 1)
                        V.tensor_copy(bb[:], group(beta[:, tc], P)).then_inc(s_rows_bcast, 1)
                        dve.wait_ge(s_row_mm, 2 * tt + 1)
                        if tt:
                            dve.wait_ge(s_lt_made, 2 * tt)
                        V.tensor_tensor(dt_[:], hd(G[2][:]), group(gcol[:, tc], P), ALU.subtract).then_inc(s_d_made, 1)
                        dve.wait_ge(s_d_made, 2 * tt + 1)
                        V.scalar_tensor_tensor(out=dt_[:], in0=dt_[:], scalar=0.0, in1=heads(C("negmask2")), op0=ALU.min,
                                               op1=ALU.add).then_inc(s_d_made, 1)
                        if tt:
                            bg.upto((tt - 1, "o", 1))
                        dve.wait_ge(s_dt_exp, tt + 1)
                        dve.wait_ge(s_kk_mm, 2 * tt + 2)
                        V.tensor_tensor(at_[:], hd(G[5][:]), dt_[:], ALU.mult).then_inc(s_at_made, 1)
                        if tt:
                            dve.wait_ge(s_bt_made, 5 * tt)
                        V.tensor_tensor(lt[:], hd(G[4][:]), dt_[:], ALU.mult).then_inc(s_lt_made, 1)
                        dve.wait_ge(s_lt_made, 2 * tt + 1)
                        dve.wait_ge(s_row_mm, 2 * tt + 2)
                        V.tensor_tensor(lt[:], lt[:], hd(G[6][:]), ALU.mult).then_inc(s_lt_made, 1)
                        dve.wait_ge(s_lt_made, 2 * tt + 2)
                        link(V.tensor_tensor(Y[:], lt[:], heads(C("lvl1")), ALU.mult))
                        V.scalar_tensor_tensor(out=Y[:], in0=Y[:], scalar=-1.0, in1=heads(C("ident")), op0=ALU.mult,
                                               op1=ALU.add).then_inc(s_y_made, 1)
                        V.tensor_tensor(bt[:], lt[:], heads(C("lvl2")), ALU.mult).then_inc(s_bt_made, 1)
                        bg.upto((tt, "rows"))
                        dve.wait_ge(s_vk_tr, 2 * tt + 2)
                        V.tensor_tensor(kb[:], hd(G[4][:]), group(beta_eg[:, tc], P), ALU.mult).then_inc(s_kb_made, 1)
                        V.tensor_tensor(kd[:], hd(G[4][:]), group(e_suf[:, tc], P), ALU.mult).then_inc(s_kb_made, 1)
                        bg.upto((tt, "vk"))
                        dve.wait_ge(s_x_tr, tt + 1)
                        V.tensor_copy(X[:], hd(G[2][:])).then_inc(s_x_made, 1)
                        V.tensor_tensor(vb[:], hd(G[5][:]), group(beta_half[:, tc], P), ALU.mult).then_inc(s_vb_made, 1)
                        dve.wait_ge(s_eg_made, tt + 1)
                        V.tensor_tensor(qg[:], qkv[:, 0:4, tok], eg[:], ALU.mult).then_inc(s_qg_made, 1)
                        bg.upto((tt, "x"))
                        for i in range(5):
                            if i < 4:
                                dve.wait_ge(s_bx_mm, 5 * tt + i + 1)
                                V.tensor_tensor(bt[:], lt[:], heads(C(f"lvl{LEVELS[i + 1]}")), ALU.mult).then_inc(s_bt_made, 1)
                                dve.wait_ge(s_yp_mm, 4 * tt + i + 1)
                                dve.wait_ge(s_x_made, 5 * tt + i + 1)
                                V.tensor_tensor(X[:], X[:], hd(G[2][:]), ALU.subtract).then_inc(s_x_made, 1)
                            dve.wait_ge(s_pty_mm, 5 * tt + i + 1)
                            dve.wait_ge(s_y_made, 6 * tt + i + 1)
                            V.tensor_tensor(Y[:], Y[:], hd(G[4][:]), ALU.subtract).then_inc(s_y_made, 1)
                            bg.upto((tt, i, 0))
                            bg.upto((tt, i, 1))
                        for c in range(2):
                            n = 2 * tt + c
                            a, b = S[:, n % 2], S[:, (n + 1) % 2]
                            dve.wait_ge(s_state, n + 1)
                            link(V.tensor_tensor(b, a, group(e_tot[c][:, tc], P), ALU.mult))
                            bg.upto((tt, "w") if c == 0 else (tt, "o", 0))
                            dve.wait_ge(s_su_mm, n + 1)
                            V.tensor_tensor(b, b, hd(G[2][:]), ALU.add).then_inc(s_state, 1)
                    def delta_output():
                        for h in range(4):
                            dve.wait_ge(s_on_r, h + 1)
                            link(V.scalar_tensor_tensor(out=rd[:, h % 2, :], in0=rd[:, h % 2, :], scalar=PAR("onorm"), in1=z_t[:, h, :],
                                                        op0=ALU.mult, op1=ALU.mult))
                            V.tensor_tensor(qkv[:, 8 + h, :], qkv[:, 8 + h, :], rd[:, h % 2, :], ALU.mult).then_inc(s_on_y, 1)
                            dve.wait_ge(s_on_y, h + 1)
                            if h == 0:
                                dve.wait_ge(s_x_spilled, 16)
                            link(V.tensor_copy(o_hi[:, h, :], qkv[:, 8 + h, :]))
                            V.tensor_tensor(o_lo[:, h, :], qkv[:, 8 + h, :], o_hi[:, h, :].bitcast(F32), ALU.subtract).then_inc(s_branch_o, 1)
                            mix_bg.upto(("on", h))
                        mix_bg.finish()

                        dve.wait_ge(s_lam_exp, 1)
                        link(V.tensor_tensor(neg_lam, lam_e[:, 1:2], lam_e[:, 0:1], ALU.subtract))
                        link(V.tensor_tensor(neg_lam, neg_lam, PAR("lambda_init"), ALU.subtract))

                    def merge(b, n, bank, gate):
                        i = b * KD + n
                        if n % 2:
                            dve.wait_ge(s_unit_used, (U_PROJ_C, U_PROJ_A, U_PROJ_B)[b] + n // 2 + 1)
                        else:
                            dve.wait_ge(s_proj_even, i // 2 + 1)
                        if b == 0:
                            dve.wait_ge(s_gate_tanh, n // 2 + 1)
                        else:
                            dve.wait_ge(s_gate2_tanh, KD * (b - 1) + n + 1)
                        if b:
                            if i - KD - 1 > 0:
                                dve.wait_ge(s_gate_out, i - KD - 1)
                        dst = gyb[:, n % 2, :] if b else merged[:, n, :]
                        V.scalar_tensor_tensor(out=dst, in0=gate[:, n, :], scalar=1.0, in1=bank[:],
                                               op0=ALU.add, op1=ALU.mult).then_inc(s_gate_merge, 1)
                        if b:
                            dve.wait_ge(s_gate_merge, i + 1)
                            V.tensor_tensor(merged[:, n, :], merged[:, n, :], gyb[:, n % 2, :], ALU.add).then_inc(s_gate_out, 1)

                    def attention(bg, maps, prob, tag, scale, out_head, between):
                        def maxima(i):
                            nk = (i % 4 + 1) * P
                            c = maps * (i % 2)
                            for m in range(maps):
                                dve.wait_ge(tag["qk"], maps * i + m + 1)
                                bank = G[2 + m] if maps == 2 else G[2 + i % 2]
                                ins = V.tensor_reduce(mx[:, c + m:c + m + 1], bank[:, 0:nk], AX.X, ALU.max)
                            link(ins)
                            if maps * (i - 1) > 0:
                                dve.wait_ge(tag["exp"], maps * (i - 1))
                            V.tensor_scalar(nm[:, c:c + maps], mx[:, c:c + maps], -scale, None, ALU.mult).then_inc(tag["nm"], 1)

                        maxima(0)
                        between()
                        for i in range(16):
                            nk = (i % 4 + 1) * P
                            c = maps * (i % 2)
                            dve.wait_ge(tag["exp"], maps * (i + 1))
                            if i > 1:
                                dve.wait_ge(tag["p"], i - 1)
                            link(V.reciprocal(rr[:, c:c + maps], rs[:, c:c + maps]))
                            if maps == 2:
                                link(V.tensor_tensor(rr[:, c + 1:c + 2], rr[:, c + 1:c + 2], neg_lam, ALU.mult))
                                link(V.tensor_scalar(prob(i, 1)[:, 0:nk], prob(i, 1)[:, 0:nk], rr[:, c + 1:c + 2], None, ALU.mult))
                                V.scalar_tensor_tensor(out=prob(i, 0)[:, 0:nk], in0=prob(i, 0)[:, 0:nk], scalar=rr[:, c:c + 1],
                                                       in1=prob(i, 1)[:, 0:nk], op0=ALU.mult, op1=ALU.add).then_inc(tag["p"], 1)
                            else:
                                V.tensor_scalar(prob(i, 0)[:, 0:nk], prob(i, 0)[:, 0:nk], rr[:, c:c + 1], None, ALU.mult).then_inc(tag["p"], 1)
                            if i:
                                bg.upto((i - 1, 2))
                            if i + 1 < 16:
                                maxima(i + 1)
                            if i % 4 == 0 and i:
                                out_head(i // 4 - 1)
                            bg.upto((i, 0))
                            bg.upto((i, 1))
                        out_head(3)

                    def diff_out(h):
                        dve.wait_ge(s_da_pv, 4 * h + 4)
                        V.tensor_copy(oraw[:, h, :], G[7][:]).then_inc(s_da_o, 1)

                    def diff_work():
                        for n in range(KD):
                            yield diff.made[("proj", 0, n)]
                            merge(0, n, G[n % 2], gates)
                        for t in range(5):
                            if t in (0, 3):
                                yield diff.made[("latsum", 4 if t else 2)]
                                dve.wait_ge(s_lat_r, 2 if t else 1)
                                dve.wait_ge(s_lat_out, 6 if t else 4)
                            wcol = PAR("qa", t) if t < 3 else PAR("kva", t - 3)
                            link(V.scalar_tensor_tensor(out=lat[:, t, :], in0=lat[:, t, :], scalar=wcol, in1=rm[:, t // 3, :],
                                                        op0=ALU.mult, op1=ALU.mult))
                            link(V.tensor_copy(lat_hi[:, t, :], lat[:, t, :]))
                            V.tensor_tensor(lat_lo[:, t, :], lat[:, t, :], lat_hi[:, t, :].bitcast(F32), ALU.subtract).then_inc(s_lat_lo, 1)

                        def rope(t):
                            dve.wait_ge(s_mqk_rot, t + 1)
                            dve.wait_ge(s_mqk_cos, t + 1)
                            link(V.tensor_tensor(my[:, t % 2, :], G[5][:], sin[:], ALU.mult))
                            V.tensor_tensor(mq[:, t, :], mq[:, t, :], my[:, t % 2, :], ALU.add).then_inc(s_mqk_rope, 1)

                        for t in range(8):
                            if t >= 2:
                                yield diff.made[("rot", t - 2)]
                                rope(t - 2)
                            yield diff.made[("sum", t)]
                            dve.wait_ge(s_mqk_r, t + 1)
                            if t > 1:
                                dve.wait_ge(s_mqk_rope, t - 1)
                            V.scalar_tensor_tensor(out=my[:, t % 2, :], in0=G[t % 2][:], scalar=PAR("mla_q" if t < 4 else "mla_k"),
                                                   in1=rm[:, t % 2, :], op0=ALU.mult, op1=ALU.mult).then_inc(s_mqk_y, 1)
                            dve.wait_ge(s_mqk_y, t + 1)
                            V.tensor_tensor(mq[:, t, :], my[:, t % 2, :], cos[:], ALU.mult).then_inc(s_mqk_cos, 1)
                        for t in (6, 7):
                            yield diff.made[("rot", t)]
                            rope(t)

                    link(V.tensor_copy(mask_row[:, 0:P], C("negmask")))
                    V.tensor_copy(mask_row[:, P:P + CHUNK], C("ones")[:, 0:CHUNK]).then_inc(s_mask_made, 1)
                    bg = Follower(diff, diff_work())
                    attention(bg, 2, lambda i, m: probs[:, i % 2, m, :], f_da, QK ** -0.5, diff_out, delta_output)
                    bg.finish()
                    def diff_output():
                        for h in range(4):
                            dve.wait_ge(s_sub_r, h + 1)
                            dve.wait_ge(s_branch_o, 4 + h - 1)
                            V.scalar_tensor_tensor(out=oy[:, h % 2, :], in0=oraw[:, h, :], scalar=subw, in1=ro[:, h % 2, :],
                                                   op0=ALU.mult, op1=ALU.mult).then_inc(s_sub_y, 1)
                            dve.wait_ge(s_sub_y, h + 1)
                            link(V.tensor_copy(o_hi[:, h, :], oy[:, h % 2, :]))
                            V.tensor_tensor(o_lo[:, h, :], oy[:, h % 2, :], o_hi[:, h, :].bitcast(F32), ALU.subtract).then_inc(s_branch_o, 1)

                    def mla_out(h):
                        dve.wait_ge(s_ma_pv, 4 * h + 4)
                        V.tensor_copy(ob_hi[:, h, :], G[7][:]).then_inc(s_ma_hi, 1)
                        dve.wait_ge(s_ma_hi, h + 1)
                        V.tensor_tensor(ob_lo[:, h, :], G[7][:], ob_hi[:, h, :].bitcast(F32), ALU.subtract).then_inc(s_ma_o, 1)

                    def mla_work():
                        for n in range(KD):
                            yield mla.made[("proj", 1, n)]
                            merge(1, n, G[4 + n % 2], gates2)

                    bg = Follower(mla, mla_work())
                    attention(bg, 1, lambda i, m: mprobs[:, i % 2, :], f_ma, MQK ** -0.5, mla_out, diff_output)
                    bg.finish()

                    def m_low(k):
                        dve.wait_ge(s_gate_out, KD + k + 1)
                        link(V.tensor_copy(m_hi[:, k, :], merged[:, k, :]))
                        V.tensor_tensor(m_lo[:, k, :], merged[:, k, :], m_hi[:, k, :].bitcast(F32), ALU.subtract).then_inc(s_m_lo, 1)

                    for n in range(KD):
                        merge(2, n, G[4 + n % 2], gates2)
                        m_low(n)
                    dve.wait_ge(s_x_back, 16)
                    for n in range(KD):
                        dve.wait_ge(s_unit_used, U_OUT + n + 1)
                        V.scalar_tensor_tensor(out=x[:, n, :], in0=G[n % 2][:], scalar=half_g[:, 0, n:n + 1], in1=x[:, n, :],
                                               op0=ALU.mult, op1=ALU.add).then_inc(s_x_mid, 1)
                        dve.wait_ge(s_x_mid, n + 1)
                        ins = V.tensor_tensor(sqx2[:] if n else ssq2[:], x[:, n, :], x[:, n, :], ALU.mult)
                        if n:
                            link(ins)
                            ins = V.tensor_tensor(ssq2[:], ssq2[:], sqx2[:], ALU.add)
                        if n < KD - 1:
                            link(ins)
                        else:
                            ins.then_inc(s_ssq, 1)
                    norm(1)

                    def hidden(j, e, first_block):
                        f = fy[:, e, :]
                        dve.wait_ge(s_ffn_tanh, j + 1)
                        if not first_block:
                            dve.wait_ge(s_ffn_lo, j - 1)
                        V.scalar_tensor_tensor(out=f, in0=ft[:, e, :], scalar=1.0, in1=G[e][:], op0=ALU.add, op1=ALU.mult).then_inc(s_ffn_y, 1)
                        dve.wait_ge(s_ffn_y, j + 1)
                        dve.wait_ge(s_unit_used, j * 2 + (U_GU + 2))
                        V.tensor_tensor(f, f, G[2 + e][:], ALU.mult).then_inc(s_ffn_y2, 1)
                        dve.wait_ge(s_ffn_y2, j + 1)
                        V.tensor_scalar(hid_hi[:, j, :], f, 1.0, None, ALU.mult).then_inc(s_ffn_hi, 1)
                        dve.wait_ge(s_ffn_hi, j + 1)
                        V.tensor_tensor(hid_lo[:, j, :], f, hid_hi[:, j, :].bitcast(F32), ALU.subtract).then_inc(s_ffn_lo, 1)

                    hidden(0, 0, True)
                    hidden(1, 1, True)
                    with dve.Fori(1, KF // 2) as i:
                        hidden(i * 2, 0, False)
                        hidden(i * 2 + 1, 1, False)

                    def residual(n, e, u_of, first_block):
                        dve.wait_ge(s_unit_used, u_of)
                        V.scalar_tensor_tensor(out=x[:, n, :], in0=G[e][:], scalar=half_g[:, 1, n:n + 1] if isinstance(n, int)
                                               else half_g[:, 1, bass.ds(n, 1)], in1=x[:, n, :], op0=ALU.mult, op1=ALU.add).then_inc(s_x_new, 1)
                        dve.wait_ge(s_x_new, n + 1)
                        first = first_block and e == 0
                        V.tensor_tensor(ssq[:] if first else sqx[:], x[:, n, :], x[:, n, :], ALU.mult).then_inc(s_x_sq, 1)
                        dve.wait_ge(s_x_sq, n + 1)
                        if not first:
                            V.tensor_tensor(ssq[:], ssq[:], sqx[:], ALU.add).then_inc(s_x_ssq, 1)
                            dve.wait_ge(s_x_ssq, n)

                    def next_ada(i):
                        for k in range(KD):
                            dve.wait_ge(s_ada2_loaded[k // 2], i * 16 + 16)
                            part = ada2[k // 2][:, k % 2, :]
                            if k == 0:
                                if not isinstance(i, int):
                                    dve.wait_ge(s_ada2_mm, i)
                                V.tensor_scalar(ada_acc2[:], part, c_col[:, 0:1], None, ALU.mult).then_inc(s_ada2_step, 1)
                            else:
                                V.scalar_tensor_tensor(out=ada_acc2[:], in0=part, scalar=c_col[:, k:k + 1], in1=ada_acc2[:],
                                                       op0=ALU.mult, op1=ALU.add).then_inc(s_ada2_step, 1)
                            dve.wait_ge(s_ada2_step, i * 8 + (k + 1))

                    def next_mod(i):
                        dve.wait_ge(s_ada2_mm, i + 1)
                        V.tensor_scalar(mod_raw[:, 4 * i:4 * i + 4] if isinstance(i, int) else mod_raw[:, bass.ds(i * 4, 4)],
                                        G[7][:, 0:4], 1.0, None, ALU.mult).then_inc(s_mod_next, 1)

                    dve.wait_ge(s_ffn_lo, KF)
                    next_ada(0)
                    residual(0, 0, U_DOWN + 3, True)
                    residual(1, 1, U_DOWN + 6, True)
                    next_mod(0)
                    with dve.Fori(1, KD // 2) as i:
                        next_ada(i)
                        residual(i * 2, 0, i * 6 + (U_DOWN + 3), False)
                        residual(i * 2 + 1, 1, i * 6 + (U_DOWN + 6), False)
                        next_mod(i)

            numbers = sorted(s.num for s in sems.values())
            assert numbers == list(range(numbers[0], numbers[0] + len(numbers)))
            nc.sync.sem_clear(range(numbers[0], numbers[-1] + 1))
            nc.all_engine_barrier()

        s_out = ctx.enter_context(nc.semaphore("out_stored"))
        with nc.Block() as last:
            @last.sync
            def _(sp):
                sp.dma_start(out, x[:]).then_inc(s_out, 16)
                sp.wait_ge(s_out, 16)


def layout(inputs):
    i = inputs
    f = np.float32

    def tiles(w, cols, width=P):
        k = w.shape[0] // P
        o = np.zeros((P, k, width), f)
        o[:, :, :cols.stop - cols.start] = w[:, cols].reshape(k, P, -1).transpose(1, 0, 2)
        return o

    widths = (512, 512, 512, 384, 288, 512, 512, 512, 512, 4, 4, 3072)
    offs = np.concatenate([[0], np.cumsum(widths)])
    a_q, a_k, a_v, b_q, b_kv, c_q, c_k, c_v, c_z, c_b, c_a, gates = offs[:12]
    wpack = np.zeros((DEPTH, UNITS_PAD, P, 8, P), f)
    apack = np.zeros((DEPTH, 4 * ADA_GROUPS, P, 2, T), f)
    params = np.zeros((DEPTH, P, NPARAM), f)
    for l in range(DEPTH):
        w_in = i["w_in"][l]
        u = [0]

        def put(block, s=0):
            wpack[l, u[0], :, s:s + block.shape[1], :] = block
            return block.shape[1]

        def step():
            u[0] += 1

        def col(a, n=P):
            put(tiles(w_in, slice(a, a + n)))
            step()

        def gate(b):
            for n in range(KD):
                col(gates + b * D + n * P)

        def project(wo):
            for n in range(KD):
                put(tiles(wo, slice(n * P, n * P + P)), 4 * (n % 2))
                if n % 2:
                    step()

        for first in (c_q, c_k, c_v, c_z):
            for t in range(4):
                col(first + t * P)
        for k in range(KD):
            put(w_in[k * P:k * P + P, a_v:a_v + T].reshape(P, 4, P), 4 * (k % 2))
            if k % 2:
                step()
        col(c_b, 8)
        for first in (a_q, a_k):
            for t in range(4):
                col(first + t * P)
        gate(2)
        project(i["w_o_gdn"][l])
        for t in range(3):
            col(b_q + t * P)
        for t in range(2):
            col(b_kv + t * P)
        rope = np.zeros((D, P), f)
        rope[:, 64:96] = w_in[:, b_kv + 256:b_kv + 288]
        put(tiles(rope, slice(0, P)))
        step()
        for h in range(4):
            put(tiles(i["mla_q_up"][l], slice(h * 96, h * 96 + 96)), 3 * (h % 2))
            if h % 2:
                step()
        for h in range(4):
            put(tiles(i["mla_kv_up"][l], slice(h * 192, h * 192 + 64)), 2 * h)
        step()
        for k in range(2):
            for h in range(4):
                put(i["mla_kv_up"][l][k * P:k * P + P, h * 192 + 64:h * 192 + 192].reshape(P, 1, P), 4 * k + h)
        step()
        gate(0)
        project(i["w_o_diff"][l])
        gate(1)
        project(i["w_o_mla"][l])
        for n in range(KD):
            put(tiles(i["w_out"][l], slice(n * P, n * P + P)))
            step()
        for j in range(KF):
            for e in range(2):
                put(tiles(i["ffn_w_gu"][l], slice(e * F + j * P, e * F + j * P + P)))
                step()
        for n in range(KD):
            for part, nk in enumerate((8, 8, 6)):
                put(tiles(i["ffn_w_down"][l][8 * part * P:(8 * part + nk) * P], slice(n * P, n * P + P)))
                step()
        assert u[0] == UNITS
        for g in range(ADA_GROUPS):
            src, group = (l, g + ADA_FIRST) if g < ADA_REST else ((l + 1) % DEPTH, g - ADA_REST)
            w = i["ada_w"][src][:, group * T:group * T + T]
            apack[l, 4 * g:4 * g + 4] = w.reshape(4, 2, P, T).transpose(0, 2, 1, 3)

        def par(name, block):
            a, b = PARAMS[name]
            params[l, :block.shape[0], a:b] = block

        par("norm1", i["norm1_w"][l].reshape(8, P).T)
        par("norm2", i["norm2_w"][l].reshape(8, P).T)
        par("ada_b", i["ada_b"][l].reshape(48, P).T)
        par("diff_q", np.concatenate([i["diff_qnorm_w"][l]] * 2)[:, None])
        par("diff_k", np.concatenate([i["diff_knorm_w"][l]] * 2)[:, None])
        par("subln", i["diff_subln_w"][l][:, None])
        par("qa", i["mla_qa_norm_w"][l].reshape(3, P).T)
        par("kva", i["mla_kva_norm_w"][l].reshape(2, P).T)
        par("mla_q", i["mla_qnorm_w"][l][:, None])
        par("mla_k", i["mla_knorm_w"][l][:, None])
        par("conv", i["gdn_conv_w"][l].reshape(4, 12, P).transpose(2, 1, 0).reshape(P, 48))
        par("onorm", i["gdn_onorm_w"][l][:, None])
        par("lambda", i["diff_lambda"][l].T)
        init = 0.8 - 0.6 * np.exp(-0.3 * l)
        par("lambda_init", np.full((P, 1), init, f))
        par("one_minus_init", np.full((P, 1), 1.0 - init, f))
        par("a_log", np.broadcast_to(np.concatenate([i["gdn_a_log"][l]] * 4), (P, 16)))
        par("dt_bias", np.broadcast_to(np.concatenate([i["gdn_dt_bias"][l]] * 4), (P, 16)))
    return wpack, apack, params


def constants():
    f = np.float32
    r = np.arange(P)
    row, col = r[:, None], r[None, :]
    same = row // CHUNK == col // CHUNK
    c = {}
    c["ident"] = np.eye(P)
    c["ones"] = np.ones((P, P))
    c["blockones"] = same
    rot = np.zeros((P, P))
    for k in range(16):
        rot[80 + k, 64 + k] = -1.0
        rot[64 + k, 80 + k] = 1.0
    c["rot"] = rot
    c["tri"] = same & (row <= col)
    c["suffix"] = same & (row > col)
    c["first"] = np.broadcast_to(row < CHUNK, (P, P))
    c["second"] = np.broadcast_to(row >= CHUNK, (P, P))
    c["negmask"] = np.where(col < CHUNK, -1e30, 0.0) * np.ones((P, P))
    c["negmask2"] = np.where(c["tri"], 0.0, -1e30)
    for s in (1, 2, 4, 8, 16, 32):
        c[f"lvl{s}"] = (row // (2 * s) == col // (2 * s)) & (col // s % 2 == 1) & (row // s % 2 == 0)
    mats = np.stack([np.asarray(c[n], f) for n in CONSTS], axis=1)
    freq = np.zeros((P, 1), f)
    inv = (f(10000.0) ** (-np.arange(16, dtype=f) / f(16))).astype(f)
    freq[64:96, 0] = np.concatenate([inv, inv])
    return np.ascontiguousarray(mats), freq


def kernel(**inputs):
    import concourse.bacc as bacc
    from concourse.bass_utils import run_bass_kernel_spmd

    inputs = {k: np.asarray(v) for k, v in inputs.items()}
    wpack, apack, params = layout(inputs)
    mats, freq = constants()
    arrays = {
        "x_in": np.ascontiguousarray(inputs["x"][0].T.reshape(KD, P, T).transpose(1, 0, 2)),
        "wpack": wpack, "apack": apack,
        "c_in": np.ascontiguousarray(inputs["c"][0].reshape(KD, P).T),
        "params": params, "consts_in": mats, "freq_in": freq,
        "pos_in": np.ascontiguousarray(inputs["positions"]),
    }
    nc = bacc.Bacc("TRN2", target_bir_lowering=False, num_devices=1)
    aps = [nc.dram_tensor(n, a.shape, mybir.dt.from_np(a.dtype), kind="ExternalInput").ap() for n, a in arrays.items()]
    out = nc.dram_tensor("out", (P, KD, T), F32, kind="ExternalOutput").ap()
    x_spill = nc.dram_tensor("x_spill", (P, KD, T), F32, kind="Internal").ap()
    x_in, wp, ap_, c_in, params_in, consts_in, freq_in, pos_in = aps
    build(nc, x_in, wp, ap_, c_in, params_in, consts_in, freq_in, pos_in, x_spill, out)
    r = run_bass_kernel_spmd(nc, [arrays], core_ids=[0])
    got = r.results[0]["out"]
    return np.ascontiguousarray(got.transpose(1, 0, 2).reshape(D, T).T)[None]
```
